# Optimizing a Trainium2 kernel written in Bass

```python
import jax, jax.numpy as jnp
from jax import lax
import numpy as np

D_MODEL = 1024
BATCH = 1
SEQ = 1024
DEPTH = 1

N_HEADS_A = 8
N_KV_HEADS_A = 2
HEAD_DIM_A = 64
GROUP_A = N_HEADS_A // N_KV_HEADS_A
N_IDX_HEADS = 4
IDX_DIM = 64
TOPK_MAX = 256
N_HEADS_B = 8
Q_LORA = 384
KV_LORA = 256
NOPE_DIM = 64
ROPE_DIM = 32
V_DIM_B = 64
ROPE_THETA = 10000.0
D_FF = 4 * D_MODEL
PLE_DIM = 256
Q_BLOCK = 128
EPS = 1e-6

IN_SIZES = (
    N_HEADS_A * HEAD_DIM_A,
    N_KV_HEADS_A * HEAD_DIM_A,
    N_KV_HEADS_A * HEAD_DIM_A,
    N_IDX_HEADS * IDX_DIM,
    IDX_DIM,
    N_IDX_HEADS,
    Q_LORA,
    KV_LORA,
    ROPE_DIM,
    D_MODEL,
    D_MODEL,
)
D_IN = sum(IN_SIZES)

kernel_name = "hybrid_dsa_mla_gated_block"

def _rmsnorm(x, g):
    xf = x.astype(jnp.float32)
    y = xf * lax.rsqrt(jnp.mean(xf * xf, axis=-1, keepdims=True) + EPS)
    return (y * g.astype(jnp.float32)).astype(x.dtype)

def _split_last(z, sizes):
    outs, start = [], 0
    for s in sizes:
        outs.append(z[..., start:start + s])
        start += s
    return outs

def _alibi_slopes(n):
    return 2.0 ** (-8.0 * jnp.arange(1, n + 1, dtype=jnp.float32) / n)

def _rope(x, positions):
    half = ROPE_DIM // 2
    inv = ROPE_THETA ** (-jnp.arange(half, dtype=jnp.float32) / half)
    ang = positions.astype(jnp.float32)[:, :, None, None] * inv
    cos, sin = jnp.cos(ang), jnp.sin(ang)
    xf = x.astype(jnp.float32)
    x1, x2 = xf[..., :half], xf[..., half:]
    out = jnp.concatenate([x1 * cos - x2 * sin, x2 * cos + x1 * sin], axis=-1)
    return out.astype(x.dtype)

def _to_blocks(a):
    b, s = a.shape[:2]
    a = a.reshape((b, s // Q_BLOCK, Q_BLOCK) + a.shape[2:])
    return jnp.moveaxis(a, 1, 0)

def _from_blocks(o):
    nb, b, qb = o.shape[:3]
    return jnp.moveaxis(o, 0, 1).reshape((b, nb * qb) + o.shape[3:])

def _dsa_attention(q, k, v, q_idx, k_idx, w_idx, positions, topk):
    b, s = q.shape[:2]
    s_idx = jnp.arange(s)
    slopes = _alibi_slopes(N_HEADS_A).reshape(N_KV_HEADS_A, GROUP_A)
    scale = HEAD_DIM_A ** -0.5

    def block(args):
        qb, qib, wb, pb, tb = args
        rel = jax.nn.relu(jnp.einsum('bqhd,bsd->bqhs', qib, k_idx))
        score = jnp.einsum('bqhs,bqh->bqs', rel, wb).astype(jnp.float32)
        causal = s_idx[None, None, :] <= tb[None, :, None]
        score = jnp.where(causal, score, -jnp.inf)
        _, sel = lax.top_k(score, topk)
        k_sel = jax.vmap(lambda kr, ir: kr[ir])(k, sel)
        v_sel = jax.vmap(lambda vr, ir: vr[ir])(v, sel)
        p_sel = jax.vmap(lambda pr, ir: pr[ir])(positions, sel)
        valid = sel <= tb[None, :, None]
        qg = qb.reshape(qb.shape[0], qb.shape[1], N_KV_HEADS_A, GROUP_A, HEAD_DIM_A)
        logits = jnp.einsum('bqcgd,bqncd->bqcgn', qg, k_sel).astype(jnp.float32) * scale
        dist = jnp.abs(pb[:, :, None] - p_sel).astype(jnp.float32)
        logits = logits - slopes[None, None, :, :, None] * dist[:, :, None, None, :]
        logits = jnp.where(valid[:, :, None, None, :], logits, -jnp.inf)
        probs = jax.nn.softmax(logits, axis=-1).astype(v.dtype)
        o = jnp.einsum('bqcgn,bqncd->bqcgd', probs, v_sel)
        return o.reshape(o.shape[0], o.shape[1], N_HEADS_A * HEAD_DIM_A)

    t_blocks = jnp.arange(s).reshape(s // Q_BLOCK, Q_BLOCK)
    out = lax.map(block, (_to_blocks(q), _to_blocks(q_idx), _to_blocks(w_idx),
                          _to_blocks(positions), t_blocks))
    return _from_blocks(out)

def _mla_attention(q, k, v):
    s = q.shape[1]
    s_idx = jnp.arange(s)
    scale = (NOPE_DIM + ROPE_DIM) ** -0.5

    def block(args):
        qb, tb = args
        logits = jnp.einsum('bqhd,bshd->bhqs', qb, k).astype(jnp.float32) * scale
        causal = s_idx[None, None, None, :] <= tb[None, None, :, None]
        logits = jnp.where(causal, logits, -jnp.inf)
        probs = jax.nn.softmax(logits, axis=-1).astype(v.dtype)
        o = jnp.einsum('bhqs,bshd->bqhd', probs, v)
        return o.reshape(o.shape[0], o.shape[1], N_HEADS_B * V_DIM_B)

    t_blocks = jnp.arange(s).reshape(s // Q_BLOCK, Q_BLOCK)
    out = lax.map(block, (_to_blocks(q), t_blocks))
    return _from_blocks(out)

def _dense(key, shape, fan_in):
    return jax.random.normal(key, shape, jnp.float32) * fan_in ** -0.5

def _gain(key, shape):
    return 1.0 + 0.02 * jax.random.normal(key, shape, jnp.float32)

def setup_inputs(seed: int = 0) -> dict:
    key = jax.random.key(seed)
    ks = jax.random.split(key, 20)
    x = jax.random.normal(ks[0], (BATCH, SEQ, D_MODEL), jnp.float32)
    p = jax.random.normal(ks[1], (DEPTH, BATCH, SEQ, PLE_DIM), jnp.float32)
    offsets = jax.random.randint(ks[2], (BATCH, 1), 0, 4096, dtype=jnp.int32)
    positions = (jnp.arange(SEQ, dtype=jnp.int32)[None, :] + offsets).astype(jnp.int32)
    L = DEPTH
    return {
        "x": x,
        "p": p,
        "positions": positions,
        "g_mix": _gain(ks[3], (L, D_MODEL)),
        "w_in": _dense(ks[4], (L, D_MODEL, D_IN), D_MODEL),
        "g_cq": _gain(ks[5], (L, Q_LORA)),
        "w_uq": _dense(ks[6], (L, Q_LORA, N_HEADS_B * (NOPE_DIM + ROPE_DIM)), Q_LORA),
        "g_ckv": _gain(ks[7], (L, KV_LORA)),
        "w_ukv": _dense(ks[8], (L, KV_LORA, N_HEADS_B * (NOPE_DIM + V_DIM_B)), KV_LORA),
        "w_pa": _dense(ks[9], (L, N_HEADS_A * HEAD_DIM_A, D_MODEL), N_HEADS_A * HEAD_DIM_A),
        "w_pb": _dense(ks[10], (L, N_HEADS_B * V_DIM_B, D_MODEL), N_HEADS_B * V_DIM_B),
        "w_out": _dense(ks[11], (L, D_MODEL, D_MODEL), D_MODEL),
        "g_mlp": _gain(ks[12], (L, D_MODEL)),
        "w_ff1": _dense(ks[13], (L, D_MODEL, D_FF), D_MODEL),
        "w_ff2": _dense(ks[14], (L, D_FF, D_MODEL), D_FF),
        "g_ple": _gain(ks[15], (L, D_MODEL)),
        "w_ple_gate": _dense(ks[16], (L, D_MODEL, D_MODEL), D_MODEL),
        "w_ple": _dense(ks[17], (L, PLE_DIM, D_MODEL), PLE_DIM),
        "g_final": _gain(ks[18], (D_MODEL,)),
    }

def reference(x, p, positions, g_mix, w_in, g_cq, w_uq, g_ckv, w_ukv, w_pa, w_pb,
              w_out, g_mlp, w_ff1, w_ff2, g_ple, w_ple_gate, w_ple, g_final):
    b, s, _ = x.shape
    topk = min(TOPK_MAX, s // 4)
    idx_scale = (N_IDX_HEADS * IDX_DIM) ** -0.5
    h = x
    for i in range(DEPTH):
        n = _rmsnorm(h, g_mix[i])
        z = n @ w_in[i]
        qa, ka, va, qi, ki, wi, cq, ckv, kr, ga, gb = _split_last(z, IN_SIZES)
        y_a = _dsa_attention(
            qa.reshape(b, s, N_HEADS_A, HEAD_DIM_A),
            ka.reshape(b, s, N_KV_HEADS_A, HEAD_DIM_A),
            va.reshape(b, s, N_KV_HEADS_A, HEAD_DIM_A),
            qi.reshape(b, s, N_IDX_HEADS, IDX_DIM),
            ki,
            wi * idx_scale,
            positions, topk)
        q_b = (_rmsnorm(cq, g_cq[i]) @ w_uq[i]).reshape(b, s, N_HEADS_B, NOPE_DIM + ROPE_DIM)
        q_b = jnp.concatenate([q_b[..., :NOPE_DIM], _rope(q_b[..., NOPE_DIM:], positions)], axis=-1)
        kv = (_rmsnorm(ckv, g_ckv[i]) @ w_ukv[i]).reshape(b, s, N_HEADS_B, NOPE_DIM + V_DIM_B)
        k_rope = jnp.broadcast_to(_rope(kr[:, :, None, :], positions), (b, s, N_HEADS_B, ROPE_DIM))
        k_b = jnp.concatenate([kv[..., :NOPE_DIM], k_rope], axis=-1)
        v_b = kv[..., NOPE_DIM:]
        y_b = _mla_attention(q_b, k_b, v_b)
        merged = jax.nn.sigmoid(ga) * (y_a @ w_pa[i]) + jax.nn.sigmoid(gb) * (y_b @ w_pb[i])
        h = h + merged @ w_out[i]
        n2 = _rmsnorm(h, g_mlp[i])
        h = h + jnp.square(jax.nn.relu(n2 @ w_ff1[i])) @ w_ff2[i]
        n3 = _rmsnorm(h, g_ple[i])
        h = h + jax.nn.sigmoid(n3 @ w_ple_gate[i]) * (p[i] @ w_ple[i])
    return _rmsnorm(h, g_final)


_drawn_inputs = setup_inputs


def setup_inputs(seed=0):
    import zlib

    import numpy as np

    out = dict(_drawn_inputs(seed))
    spreads = {}
    factors = {'g_cq': 8.0, 'g_ckv': 8.0, 'g_mlp': 3.407, 'g_ple': 8.0, 'g_final': 2.895}
    for name, (base, spread) in spreads.items():
        noise = np.random.default_rng([zlib.crc32(name.encode()), seed]).standard_normal(out[name].shape)
        drawn = base * np.exp(spread * noise) if base else spread * noise
        out[name] = __import__('jax').numpy.asarray(drawn.astype(out[name].dtype))
    for name, factor in factors.items():
        out[name] = (out[name] * factor).astype(out[name].dtype)
    return out
```

```python
from contextlib import ExitStack

import concourse.bass as bass
from concourse import mybir

P = 128
F32 = mybir.dt.float32
F32R = mybir.dt.float32r
BF16 = mybir.dt.bfloat16
I32 = mybir.dt.int32
ALU = mybir.AluOpType
ACT = mybir.ActivationFunctionType
AXIS = mybir.AxisListType

HEADS, HEAD_DIM = 8, 64
KV_HEADS_A = 2
IDX_HEADS = 4
TOPK = 256
NOPE, ROPE = 64, 32
THETA = 10000.0
EPS = 1e-6
NEG = -1e30
LOWEST = -3e38
SCALE_A = HEAD_DIM ** -0.5
SCALE_B = (NOPE + ROPE) ** -0.5
ROUND_MAGIC = 1.5 * 2 ** 23
TWO_PI_1 = 6.28125
TWO_PI_2 = 0.0019350051879882812
TWO_PI_3 = 3.019916050561733e-07
PI = 3.1415925
KT, WCOL = 4, 256
SLAB = KT * WCOL


class Place:

    def __init__(self):
        self.slabs = self.groups = self.turns = 0
        self.i, self.per = None, (0, 0, 0)

    def loop(self, i, slabs=0, groups=0, turns=0):
        assert slabs % 2 == 0 and groups % 2 == 0
        self.i, self.per = i, (slabs, groups, turns)
        self.start = (self.slabs, self.groups, self.turns)

    def end(self, trips):
        now = (self.slabs, self.groups, self.turns)
        assert tuple(n - s for n, s in zip(now, self.start)) == self.per, (now, self.start, self.per)
        self.slabs, self.groups, self.turns = (n + p * (trips - 1) for n, p in zip(now, self.per))
        self.i, self.per = None, (0, 0, 0)

    def value(self, first, per):
        return first if self.i is None or per == 0 else self.i * per + first

    def slab(self):
        n, per = self.slabs, self.per[0]
        self.slabs += 1
        return n % 2, n, self.value(n, per), self.value(16 * (n // 2 + 1), 8 * per)

    def group(self, slabs=0, turn=False):
        n, per = self.groups, self.per[1]
        self.groups += 1
        self.slabs += slabs
        if turn or not slabs:
            self.turns += 1
            done = ("turn", self.value(self.turns, self.per[2]))
        else:
            done = ("slab", self.value(self.slabs, self.per[0]))
        return n % 2, done, self.value(n // 2, per // 2), self.value(n // 2 + 1, per // 2)


def build(nc, x, p, positions, g_mix, w_in, g_cq, w_uq, g_ckv, w_ukv, w_pa, w_pb, w_out, g_mlp, w_ff1, w_ff2,
          g_ple, w_ple_gate, w_ple, g_final, out):
    _, S, D = x.shape
    FF = w_ff1.shape[2]
    QL, KVL, PL = w_uq.shape[1], w_ukv.shape[1], w_ple.shape[1]
    TT = S // P
    DT = D // P
    QT, KVT = QL // P, KVL // P
    HALF = S // 2
    HD = HEADS * HEAD_DIM
    YT = HD // P
    QI0 = HD + 2 * KV_HEADS_A * HEAD_DIM
    KI0 = QI0 + IDX_HEADS * HEAD_DIM
    CQ0 = KI0 + HEAD_DIM + IDX_HEADS
    KR0 = CQ0 + QL + KVL
    G0 = KR0 + ROPE
    QB_DIM = NOPE + ROPE
    assert (S, D) == (1024, 1024) and QT == 3 and KVT == 2
    GATES_N = 2 * D // (2 * WCOL)
    OUT_N = D // (2 * WCOL)
    CHUNK = 4
    FFN = FF // (CHUNK * P)
    KEYS = [(i + 1) * P for i in range(TT)]
    SC_AT = [sum(KEYS[:i]) for i in range(TT)]
    SELECT_FROM = TOPK // P

    x2, p2, out2 = x[0], p[0, 0], out[0]
    wi, uq, ukv, pa, pb, wo = w_in[0], w_uq[0], w_ukv[0], w_pa[0], w_pb[0], w_out[0]
    f1, f2, pg, pw = w_ff1[0], w_ff2[0], w_ple_gate[0], w_ple[0]
    gates_d = nc.dram_tensor("gates_scratch", (2 * D // P, P, S), F32, kind="Internal").ap()
    rope_d = nc.dram_tensor("rope_scratch", (2, ROPE, S), F32, kind="Internal").ap()

    ctx = ExitStack()
    with ctx:
        K = 1024
        base = (nc.sbuf_base + 31) // 32 * 32

        def at(name, off, shape, dt=F32):
            return nc.alloc_sbuf_tensor_at(name, [P] + shape, dt, offset=base + off)

        W_AT, NX, R1, R2, T = 0, 24 * K, 88 * K, 136 * K, 182 * K
        MISC = 198 * K
        w_raw = [at(f"w_raw{s}", W_AT + s * 4 * K, [KT, WCOL]) for s in range(2)]
        w_hi = [at(f"w_hi{s}", W_AT + (8 + s * 4) * K, [KT, WCOL], F32R) for s in range(2)]
        w_lo = [at(f"w_lo{s}", W_AT + (16 + s * 4) * K, [KT, WCOL], F32R) for s in range(2)]
        n_hi, n_lo = at("n_hi", NX, [DT, S], F32R), at("n_lo", NX + 32 * K, [DT, S], F32R)
        qb, kvb = at("qb", NX, [HEADS, S]), at("kvb", NX + 32 * K, [HEADS, S])
        merged_hi = at("merged_hi", NX, [DT, S], F32R)
        ya_hi, ya_lo = at("ya_hi", NX + 32 * K, [YT, S], F32R), at("ya_lo", NX + 48 * K, [YT, S], F32R)
        x_tok = at("x_tok", R1, [TT, D])
        qi = at("qi", R1, [2, S])
        ki = at("ki", R1 + 8 * K, [S])
        ki_wi = at("ki_wi", R1 + 12 * K, [S])
        rel = at("rel", R1 + 16 * K, [2, S])
        ckv_hi, ckv_lo = at("ckv_hi", R1, [KVT, S], F32R), at("ckv_lo", R1 + 8 * K, [KVT, S], F32R)
        cq_hi, cq_lo = at("cq_hi", R1 + 16 * K, [QT, S], F32R), at("cq_lo", R1 + 28 * K, [QT, S], F32R)
        rms_c = at("rms_c", R1 + 40 * K, [2, S])
        vb = at("vb", R1, [TT, HD])
        yb_hi, yb_lo = at("yb_hi", R1 + 16 * K, [YT, S], F32R), at("yb_lo", R1 + 32 * K, [YT, S], F32R)
        h = at("h", R1, [DT, S])
        sc = at("sc", R2, [sum(KEYS)])
        qa = at("qa", R2 + 18 * K, [YT, S])
        ka = at("ka", R2 + 34 * K, [KV_HEADS_A, S])
        va = at("va", R2 + 42 * K, [TT, P])
        gmix_row = at("gmix_row", R2, [D])
        merged_lo = at("merged_lo", R2, [DT, S], F32R)
        gated = at("gated", R2 + 32 * K, [2, S])
        hid_hi, hid_lo = at("hid_hi", R2, [CHUNK, S], F32R), at("hid_lo", R2 + 16 * K, [CHUNK, S], F32R)
        p_tok = at("p_tok", R1 + 32 * K, [TT, PL])
        pt_hi, pt_lo = at("pt_hi", R2, [2, S], F32R), at("pt_lo", R2 + 8 * K, [2, S], F32R)
        tk_work, tk_eq, tk_rank = at("tk_work", T, [S]), at("tk_eq", T + 4 * K, [S]), at("tk_rank", T + 8 * K, [S])
        stage = at("stage", T + 12 * K, [S])
        rope_a = at("rope_a", T, [S])
        rope_k = at("rope_k", T + 4 * K, [S])
        rope_r = at("rope_r", T + 8 * K, [S])
        rope_cos, rope_sin = at("rope_cos", R1 + 16 * K, [S]), at("rope_sin", R1 + 20 * K, [S])
        swap = [at(f"swap{b}", R1 + (24 + 4 * b) * K, [S]) for b in range(4)]
        kr = at("kr", T + 12 * K, [S])
        prob = at("prob", T, [2, S])
        prob_t = at("prob_t", T + 8 * K, [2, S])
        sig_ab = at("sig_ab", T, [2, 2, S])
        xs = at("xs", T, [2, TT, WCOL])
        tmp = at("tmp", T, [2, 2, S])
        pos_f = at("pos_f", MISC, [S])
        rms = at("rms", MISC, [S])
        c32 = at("c32", MISC + 4 * K, [S])
        y_f32 = at("y_f32", MISC + 4 * K, [2, HD])
        sq_sum = at("sq_sum", MISC + 4 * K, [S])
        gfin_row = at("gfin_row", MISC + 4 * K, [D])
        m = MISC + 8 * K
        ident = at("ident", m, [P])
        ones = at("ones", m + 512, [P])
        ident_b = at("ident_b", m + 1024, [P], BF16)
        causal_b = at("causal_b", m + 1280, [P], BF16)
        small = m + 1536
        COLS = 92
        assert base + small + 4 * COLS <= nc.sbuf_usable_end
        cols = at("cols", small, [COLS])
        names = {}

        def col(name, n=1):
            at0 = names.setdefault(name, (sum(v[1] for v in names.values()), n))[0]
            assert at0 + n <= COLS
            return cols[:, at0:at0 + n]

        g_cq_c, g_ckv_c = col("g_cq", QT), col("g_ckv", KVT)
        g_mlp_c, g_ple_c = col("g_mlp", DT), col("g_ple", DT)
        eps_c = col("eps")
        q_scale = col("q_scale", YT)
        inv_c = col("inv", 2)
        ss_c = col("ss", 2)
        rstd_c = col("rstd", 2)
        top8 = col("top8", 8)
        need_c = col("need")
        max_c = col("max", 4)
        shift_c = col("shift", 4)
        sums = col("sums", 2 * HEADS)
        inv_sum = col("inv_sum", HEADS)
        neg_pos = col("neg_pos", TT)
        q_norm = col("q_norm", TT)
        w_tok = at("w_tok", R1 + 32 * K, [TT, IDX_HEADS])
        pos_i = at("pos_i", R1 + 33 * K, [S], I32)
        pos_ci = at("pos_ci", R1 + 37 * K, [TT], I32)
        rows = at("rows", R1 + 38 * K, [2, P])

        ps = ctx.enter_context(nc.psum_tensor("ps", [P, 8, HALF], F32))

        def bank(b, n=1):
            return ps[:, b:b + n, :].rearrange("p b n -> p (b n)")

        def tile_ps(half, j, n=1):
            return bank(4 * half + 2 * j, 2 * n)

        def sem(name):
            return ctx.enter_context(nc.semaphore(name))

        raw_loaded = [sem("raw_loaded0"), sem("raw_loaded1")]
        hi_ready, lo_ready = sem("hi_ready"), sem("lo_ready")
        slab_used, turn_done = sem("slab_used"), sem("turn_done")
        psum_free = [sem("psum_free0"), sem("psum_free1")]
        x_loaded = [sem(f"x_loaded{t}") for t in range(DT)]
        xs_loaded = [sem("xs_loaded0"), sem("xs_loaded1")]
        stored = [sem("stored0"), sem("stored1")]
        const_cols = sem("const_cols")
        consts_half = sem("consts_half")
        consts_ready = sem("consts_ready")
        row_ready = sem("row_ready")
        gains_loaded = sem("gains_loaded")
        pos_loaded = sem("pos_loaded")
        row_ss = sem("row_ss")
        row_std = sem("row_std")
        x_scaled = sem("x_scaled")
        n_hi_done = sem("n_hi_done")
        col_done = sem("col_done")
        rope_arg = sem("rope_arg")
        rope_saved = sem("rope_saved")
        idx_ready = sem("idx_ready")
        ki_copied = sem("ki_copied")
        wi_done = sem("wi_done")
        wi_copied = sem("wi_copied")
        idx_done = sem("idx_done")
        rel_done = sem("rel_done")
        rel_used = sem("rel_used")
        near_dist = sem("near_dist")
        sq_pair = sem("sq_pair")
        far_masked = sem("far_masked")
        near_masked = sem("near_masked")
        dist_ready = sem("dist_ready")
        ka_ready = sem("ka_ready")
        ka_copied = sem("ka_copied")
        c_scaled = sem("c_scaled")
        c_sq = sem("c_sq")
        c_hi = sem("c_hi")
        c_lo = sem("c_lo")
        c_sum = sem("c_sum")
        gate_ready = sem("gate_ready")
        gate_saved = sem("gate_saved")
        table_loaded = sem("table_loaded")
        swap_loaded = [sem(f"swap_loaded{b}") for b in range(4)]
        rope_done = [sem("rope_done_pool"), sem("rope_done_dve")]
        latent_inv = sem("latent_inv")
        q_norm_turned = sem("q_norm_turned")
        kv_scaled = sem("kv_scaled")
        kr_copied = sem("kr_copied")
        s_ready = sem("s_ready")
        shift_ready = sem("shift_ready")
        prob_ready = sem("prob_ready")
        pt_ready = sem("pt_ready")
        pt_dve = sem("pt_dve")
        pt_act = sem("pt_act")
        pv_done = sem("pv_done")
        y_factor_ready = sem("y_factor_ready")
        y_ready = sem("y_ready")
        yt_ready = sem("yt_ready")
        y_hi_done = sem("y_hi_done")
        y_split = sem("y_split")
        sig_loaded = sem("sig_loaded")
        gated_ready = sem("gated_ready")
        m_hi_done = sem("m_hi_done")
        m_lo_done = sem("m_lo_done")
        h_sq = sem("h_sq")
        sq_ready = sem("sq_ready")
        rms_std = sem("rms_std")
        norm_hi = sem("norm_hi")
        norm_lo = sem("norm_lo")
        relu_ready = sem("relu_ready")
        hid_sq = sem("hid_sq")
        hid_hi_done = sem("hid_hi_done")
        hid_lo_done = sem("hid_lo_done")
        p_loaded = sem("p_loaded")
        pt_hi_done = sem("pt_hi_done")
        gate_in = sem("gate_in")
        gate_fn = sem("gate_fn")
        h_final = sem("h_final")
        gfin_loaded = sem("gfin_loaded")
        fin_ss = sem("fin_ss")
        fin_std = sem("fin_std")
        dve_step = sem("dve_step")
        act_step = sem("act_step")

        def complete(eng, done):
            eng.wait_ge(turn_done if done[0] == "turn" else slab_used, done[1])

        def freed(eng, half, count):
            if not isinstance(count, int) or count > 0:
                eng.wait_ge(psum_free[half], count)

        def wt(w, k0, nk, c0, n):
            return w[k0 * P:(k0 + nk) * P, :].rearrange("(k q) c -> q k c", q=P)[:, :, bass.ds(c0, n)]

        VA_GROUP = TT + 6
        SUM_GROUP = VA_GROUP + 3
        KR_GROUP = SUM_GROUP + 1 + 2 * GATES_N
        LATENT_HEADS = [("kv", g) for g in range(HEADS // 2)]
        for g in range(HEADS // 2):
            LATENT_HEADS += [("q", g), ("vt", g)]
        KV_GROUP, UQ_GROUP, VT_GROUP = ([KR_GROUP + 1 + LATENT_HEADS.index((kind, g)) for g in range(HEADS // 2)]
                                        for kind in ("kv", "q", "vt"))
        OUT_GROUP = KR_GROUP + 1 + len(LATENT_HEADS) + DT
        PT_GROUP = OUT_GROUP + 2 * OUT_N + 1 + 6 * FFN
        FIN_GROUP = PT_GROUP + 1 + 4 * OUT_N + 1
        SQ3 = 2 * OUT_N + 1
        SLOPES = [2.0 ** (-8.0 * (hd + 1) / HEADS) for hd in range(HEADS)]
        LATENTS = [(cq_lo[:, k, :], cq_hi[:, k, :], rms_c[:, 0, :], k == 0, max(k - 1, 0), g_cq_c[:, k:k + 1])
                   for k in range(QT)]
        LATENTS += [(ckv_lo[:, k, :], ckv_hi[:, k, :], rms_c[:, 1, :], k == 0, QT - 1, g_ckv_c[:, k:k + 1])
                    for k in range(KVT)]

        def free_count(g):
            return g // 2 + 1

        ROPES = [kr] + [qb[:, hd, :] for hd in range(HEADS)]
        POOL_ROPES = 3

        def rope_place(n):
            return (0, n) if n < POOL_ROPES else (1, n - POOL_ROPES)

        def rope(eng, n):
            e, m = rope_place(n)
            b = 2 * e + m % 2
            rows_, sw = ROPES[n][NOPE:QB_DIM, :], swap[b][NOPE:QB_DIM, :]
            done = rope_done[e]
            eng.wait_ge(swap_loaded[b], 32 * (m // 2 + 1))
            eng.tensor_tensor(sw, sw, rope_sin[NOPE:QB_DIM, :], ALU.mult).then_inc(done, 1)
            eng.tensor_tensor(rows_, rows_, rope_cos[NOPE:QB_DIM, :], ALU.mult).then_inc(done, 1)
            eng.wait_ge(done, 3 * m + 2)
            eng.tensor_tensor(rows_, rows_, sw, ALU.add).then_inc(done, 1)

        STEPS = [(br, i, hd) for br in "BA" for i in range(TT) for hd in range(HEADS)]
        N = len(STEPS)
        BANK_BLOCKS = HALF // P

        def copied(n):
            _, i, hd = STEPS[n]
            if i >= BANK_BLOCKS:
                return (BANK_BLOCKS, i + 1), (0, BANK_BLOCKS)
            return ((0, i + 1), None) if hd % 2 == 0 else (None, (0, i + 1))

        def copies(engine, n):
            return sum(1 for k in range(n) if copied(k)[engine])

        block = ctx.enter_context(nc.Block())

        @block.sync
        def _(sp):
            at_ = Place()

            def load(src, nk=KT, n=WCOL):
                s, first, num, _ = at_.slab()
                if first >= 2:
                    sp.wait_ge(lo_ready, num - 1)
                sp.dma_start(w_raw[s][:, 0:nk, 0:n], src).then_inc(raw_loaded[s], 16)

            def load_kn(w, c0, n=WCOL):
                for k0 in (0, KT):
                    load(wt(w, k0, KT, c0, n), KT, n)

            sp.dma_start(x_tok[:, 0, :], x2[0:P, :]).then_inc(x_loaded[0], 16)
            sp.dma_start(gmix_row[:, :], g_mix[0].partition_broadcast(P)).then_inc(gains_loaded, 16)
            for t in range(1, TT):
                sp.dma_start(x_tok[:, t, :], x2[t * P:(t + 1) * P, :]).then_inc(x_loaded[t], 16)
            sp.dma_start(pos_i[:, :], positions[0].partition_broadcast(P)).then_inc(pos_loaded, 16)
            load_kn(wi, QI0)
            load_kn(wi, KI0, HEAD_DIM + IDX_HEADS)
            load_kn(wi, 0)
            sp.wait_ge(idx_ready, 1)
            sp.dma_start(ki[HEAD_DIM:P, :], ki[0:HEAD_DIM, :]).then_inc(ki_copied, 16)
            load_kn(wi, WCOL)
            load_kn(wi, HD)
            load_kn(wi, CQ0)
            sp.wait_ge(ka_ready, 2)
            sp.dma_start(ka[HEAD_DIM:P, 0, :], ka[0:HEAD_DIM, 0, :]).then_inc(ka_copied, 16)
            sp.dma_start(ka[0:HEAD_DIM, 1, :], ka[HEAD_DIM:P, 1, :]).then_inc(ka_copied, 16)
            load_kn(wi, CQ0 + WCOL)
            load_kn(wi, CQ0 + 2 * WCOL, P)
            with sp.Fori(0, GATES_N) as i:
                at_.loop(i, 4, 0)
                for j in range(2):
                    load_kn(wi, i * (2 * WCOL) + (G0 + j * WCOL))
                at_.end(GATES_N)
            load_kn(wi, KR0 - NOPE, QB_DIM)
            for g in range(HEADS // 2):
                load(wt(ukv, 0, KVT, g * WCOL, WCOL), KVT)
            for g in range(HEADS // 2):
                load(wt(uq, 0, QT, g * 2 * QB_DIM, 2 * QB_DIM), QT, 2 * QB_DIM)
            load(wt(pa, 0, KT, 0, WCOL))
            load(wt(pb, 0, KT, 0, WCOL))
            sp.wait_ge(rope_saved, 32)
            for g in range(HEADS // 2):
                freed(sp, UQ_GROUP[g] % 2, free_count(UQ_GROUP[g]))
            freed(sp, KR_GROUP % 2, free_count(KR_GROUP))
            lo, mid, hi = NOPE, NOPE + ROPE // 2, QB_DIM
            sp.dma_start(rope_cos[lo:hi, :], rope_d[0]).then_inc(table_loaded, 16)
            sp.dma_start(rope_sin[lo:hi, :], rope_d[1]).then_inc(table_loaded, 16)

            def swap_halves(n):
                e, m = rope_place(n)
                b = 2 * e + m % 2
                if m >= 2:
                    sp.wait_ge(rope_done[e], 3 * (m - 1))
                sp.dma_start(swap[b][lo:mid, :], ROPES[n][mid:hi, :]).then_inc(swap_loaded[b], 16)
                sp.dma_start(swap[b][mid:hi, :], ROPES[n][lo:mid, :]).then_inc(swap_loaded[b], 16)

            for n in (0, POOL_ROPES, 1, POOL_ROPES + 1):
                swap_halves(n)
            sp.wait_ge(rope_done[0], 3)
            for g in range(HEADS // 2):
                freed(sp, VT_GROUP[g] % 2, free_count(VT_GROUP[g]))
                for hd in (2 * g, 2 * g + 1):
                    sp.dma_start(kvb[lo:hi, hd, :], kr[lo:hi, :]).then_inc(kr_copied, 16)
            for n in [2] + list(range(POOL_ROPES + 2, HEADS + 1)):
                swap_halves(n)

            def load_gates(i):
                for br in range(2):
                    sp.dma_start(sig_ab[:, br, :, :],
                                 gates_d[bass.ds(i * 2 + br * DT, 2)].rearrange("a q n -> q a n")
                                 ).then_inc(sig_loaded, 16)

            sp.wait_ge(gate_saved, 16 * 2 * DT)
            sp.wait_ge(y_split, 2 * TT)
            load_gates(0)
            with sp.Fori(0, DT // 2 - 1) as i:
                at_.loop(i, 2, 0)
                load(wt(pa, 0, KT, (i + 1) * WCOL, WCOL))
                load(wt(pb, 0, KT, (i + 1) * WCOL, WCOL))
                sp.wait_ge(gated_ready, i + 1)
                load_gates(i + 1)
                at_.end(DT // 2 - 1)
            for q in range(2 * OUT_N):
                load_kn(wo, q * WCOL)
                if q < 2:
                    sp.wait_ge(gated_ready, DT // 2)
                else:
                    freed(sp, (OUT_GROUP + q - 2) % 2, free_count(OUT_GROUP + q - 2))
                sp.dma_start(xs[:, q % 2, :, :], x2.rearrange("(t q) d -> q t d", q=P)
                             [:, :, q * WCOL:(q + 1) * WCOL]).then_inc(xs_loaded[q % 2], 16)
            sp.dma_start(p_tok[:, :, :], p2.rearrange("(t q) d -> q t d", q=P)).then_inc(p_loaded, 16)
            with sp.Fori(0, FFN) as i:
                at_.loop(i, 8, 0)
                for j in range(2):
                    load_kn(f1, i * (CHUNK * P) + j * WCOL)
                for j in range(4):
                    load(f2[bass.ds(i * (CHUNK * P), CHUNK * P), j * WCOL:(j + 1) * WCOL]
                         .rearrange("(k q) c -> q k c", q=P))
                at_.end(FFN)
            for q in range(2 * OUT_N):
                load_kn(pg, q * WCOL)
                load(wt(pw, 0, 2, q * WCOL, WCOL), 2)
            sp.wait_ge(rms_std, 2)
            sp.dma_start(gfin_row[:, :], g_final.partition_broadcast(P)).then_inc(gfin_loaded, 16)
            for t in range(TT):
                g = FIN_GROUP + t
                freed(sp, g % 2, free_count(g))
                sp.dma_start(out2[t * P:(t + 1) * P, :], tmp[:, t % 2, 0, :]).then_inc(stored[t % 2], 16)
            for s in range(2):
                sp.wait_ge(stored[s], 16 * TT // 2)

        @block.gpsimd
        def _(pool):
            at_ = Place()
            with nc.allow_non_contiguous_dma(reason="gain and position columns, one float per partition"):
                for c, g in ((g_cq_c, g_cq[0]), (g_ckv_c, g_ckv[0]), (g_mlp_c, g_mlp[0]), (g_ple_c, g_ple[0])):
                    pool.dma_start(c, g.rearrange("(k q) -> q k", q=P)).then_inc(const_cols, 16)
                pool.dma_start(pos_ci[:, :], positions[0].rearrange("(t q) -> q t", q=P)).then_inc(const_cols, 16)
            for tl in (ident, ident_b, causal_b):
                pool.memset(tl[:, :], 0.0).then_inc(consts_half, 1)
            pool.memset(ones[:, :], 1.0).then_inc(consts_ready, 1)
            pool.wait_ge(consts_half, 3)
            for tl in (ident, ident_b):
                pool.affine_select(out=tl[:, :], in_=tl[:, :], compare_op=ALU.not_equal, fill=1.0, base=0,
                                   pattern=[[-1, P]], channel_multiplier=1).then_inc(consts_ready, 1)
            pool.affine_select(out=causal_b[:, :], in_=causal_b[:, :], compare_op=ALU.is_ge, fill=NEG, base=0,
                               pattern=[[-1, P]], channel_multiplier=1).then_inc(consts_ready, 1)

            def lo_parts(k):
                for _ in range(k):
                    s, _, num, _ = at_.slab()
                    pool.wait_ge(hi_ready, num + 1)
                    pool.tensor_tensor(w_lo[s][:, :, :], w_raw[s][:, :, :], w_hi[s][:, :, :].bitcast(F32),
                                       ALU.subtract).then_inc(lo_ready, 1)

            lo_parts(2)
            pool.wait_ge(near_dist, SELECT_FROM)
            for i in range(SELECT_FROM):
                diag = sc[:, SC_AT[i] + i * P:SC_AT[i] + KEYS[i]]
                pool.affine_select(out=diag, in_=diag, compare_op=ALU.is_ge, fill=-NEG, base=0,
                                   pattern=[[-1, P]], channel_multiplier=1).then_inc(near_masked, 1)
            lo_parts(4)
            for i in range(SELECT_FROM, TT):
                diag = sc[:, SC_AT[i] + i * P:SC_AT[i] + KEYS[i]]
                pool.wait_ge(rel_used, IDX_HEADS * (i - SELECT_FROM + 1))
                pool.affine_select(out=diag, in_=diag, compare_op=ALU.is_ge, fill=LOWEST, base=0,
                                   pattern=[[-1, P]], channel_multiplier=1).then_inc(far_masked, 1)
            lo_parts(8)

            def latent_lo(c):
                dst_lo, dst_hi, total, first = LATENTS[c][0:4]
                pool.wait_ge(c_hi, c + 1)
                pool.tensor_tensor(dst_lo, c32[:, :], dst_hi.bitcast(F32), ALU.subtract).then_inc(c_lo, 1)
                if not first:
                    k = LATENTS[c][4]
                    pool.wait_ge(c_sq, c + 1)
                    if k >= 1:
                        pool.wait_ge(c_sum, k)
                    pool.tensor_tensor(total, total, stage[:, :], ALU.add).then_inc(c_sum, 1)

            latent_lo(0)
            latent_lo(1)
            lo_parts(2)
            latent_lo(2)
            latent_lo(3)
            lo_parts(2)
            latent_lo(4)

            def lo_loop(trips, n):
                with pool.Fori(0, trips) as i:
                    at_.loop(i, n, 0)
                    lo_parts(n)
                    at_.end(trips)

            lo_loop(GATES_N, 4)
            lo_parts(HEADS // 2)
            pool.wait_ge(latent_inv, 1)
            for g in range(HEADS // 2):
                freed(pool, KV_GROUP[g] % 2, free_count(KV_GROUP[g]))
                pair = kvb[:, 2 * g:2 * g + 2, :]
                pool.tensor_tensor(pair, pair, rms_c[:, 1, :].unsqueeze(1).to_broadcast([P, 2, S]),
                                   ALU.mult).then_inc(kv_scaled, 1)
                lo_parts(1)
            pool.wait_ge(table_loaded, 32)
            pool.wait_ge(lo_ready, at_.slabs)
            for n in range(POOL_ROPES):
                rope(pool, n)
            pool.wait_ge(rope_done[0], 3 * POOL_ROPES)
            for trips, n in ((DT // 2, 2), (OUT_N, 4), (FFN, 8), (OUT_N, 6)):
                lo_loop(trips, n)

        @block.scalar
        def _(act):
            at_ = Place()
            ahead = Place()
            steps = [0]

            def link(ins):
                steps[0] += 1
                ins.then_inc(act_step, 1)
                act.wait_ge(act_step, steps[0])

            def hi_parts(k):
                for _ in range(k):
                    s, first, num, filled = ahead.slab()
                    act.wait_ge(raw_loaded[s], filled)
                    if first >= 2:
                        act.wait_ge(slab_used, num - 1)
                    act.activation(w_hi[s][:, :, :], w_raw[s][:, :, :], ACT.Copy).then_inc(hi_ready, 1)

            def group(slabs=0):
                half, done, _, free = at_.group(slabs)
                complete(act, done)
                return half

            def x_hi(t):
                half = group()
                act.activation(n_hi[:, :, t * P:(t + 1) * P],
                               bank(4 * half, 2).rearrange("q (k n) -> q k n", k=DT), ACT.Copy).then_inc(n_hi_done, 1)

            for t in range(TT):
                act.wait_ge(x_loaded[t], 16)
                if t >= 2:
                    act.wait_ge(x_scaled, t - 1)
                act.activation(stage[:, :], x_tok[:, t, :], ACT.Square,
                               accum_out=ss_c[:, t % 2:t % 2 + 1]).then_inc(row_ss, 1)
                act.wait_ge(row_ss, t + 1)
                if t == 0:
                    act.wait_ge(row_ready, 1)
                act.activation(rstd_c[:, t % 2:t % 2 + 1], ss_c[:, t % 2:t % 2 + 1], ACT.Sqrt,
                               bias=eps_c, scale=1.0 / D).then_inc(row_std, 1)
                if t >= 1:
                    x_hi(t - 1)
            x_hi(TT - 1)
            hi_parts(2)
            lo, hi = NOPE, QB_DIM
            act.wait_ge(rope_arg, 1)
            link(act.activation(rope_r[lo:hi, :], rope_r[lo:hi, :], ACT.Sin))
            act.dma_start(rope_d[0], rope_r[lo:hi, :]).then_inc(rope_saved, 16)
            act.wait_ge(rope_arg, 2)
            link(act.activation(stage[lo:hi, :], stage[lo:hi, :], ACT.Sin, scale=inv_c[lo:hi, 1:2]))
            act.dma_start(rope_d[1], stage[lo:hi, :]).then_inc(rope_saved, 16)
            hi_parts(2)
            half = group(2)
            act.activation(qi[:, :, :].rearrange("q a n -> q (a n)"), bank(4 * half, 4), ACT.Copy).then_inc(
                psum_free[half], 1)
            hi_parts(2)
            half = group(2)
            wr = slice(HEAD_DIM, HEAD_DIM + IDX_HEADS)
            act.activation(ki[0:HEAD_DIM, :], tile_ps(half, 0)[0:HEAD_DIM, :], ACT.Copy).then_inc(idx_ready, 1)
            act.activation(ki_wi[wr, :], tile_ps(half, 0)[wr, :], ACT.Copy).then_inc(psum_free[half], 1)
            m = 0
            for i in range(SELECT_FROM, TT):
                for hd in range(IDX_HEADS):
                    act.wait_ge(idx_done, m + 1)
                    if m >= 2:
                        act.wait_ge(rel_used, m - 1)
                    act.activation(rel[:, m % 2, 0:KEYS[i]], bank(2 * (m % 4), 2)[:, 0:KEYS[i]],
                                   ACT.Relu).then_inc(rel_done, 1)
                    m += 1
            for g in range(2):
                hi_parts(2)
                half = group(2)
                for j in range(2):
                    last = act.activation(qa[:, 2 * g + j, :], tile_ps(half, j), ACT.Copy,
                                          scale=q_scale[:, 2 * g + j:2 * g + j + 1])
                last.then_inc(psum_free[half], 1)
            hi_parts(2)
            half = group(2)
            for c in range(KV_HEADS_A):
                r = slice(c * HEAD_DIM, (c + 1) * HEAD_DIM)
                act.activation(ka[r, c, :], tile_ps(half, 0)[r, :], ACT.Copy).then_inc(ka_ready, 1)
            act.activation(c32[:, :], tile_ps(half, 1), ACT.Copy).then_inc(psum_free[half], 1)

            def latent(c, src, last):
                dst_hi, total, first, gain = LATENTS[c][1], LATENTS[c][2], LATENTS[c][3], LATENTS[c][5]
                if c == 0:
                    act.wait_ge(turn_done, TT + 1)
                    act.wait_ge(rel_used, IDX_HEADS * (TT - SELECT_FROM))
                    act.wait_ge(rope_saved, 32)
                else:
                    act.wait_ge(c_lo, c)
                if not first and LATENTS[c][4] >= 1:
                    act.wait_ge(c_sum, LATENTS[c][4])
                act.activation(total if first else stage[:, :], src, ACT.Square).then_inc(c_sq, 1)
                ins = act.activation(c32[:, :], src, ACT.Copy, scale=gain)
                if last is None:
                    ins.then_inc(c_scaled, 1)
                    act.wait_ge(c_scaled, c // 2 + 1)
                else:
                    ins.then_inc(psum_free[last], 1)
                    freed(act, last, (at_.groups - 1) // 2 + 1)
                act.activation(dst_hi, c32[:, :], ACT.Copy).then_inc(c_hi, 1)

            hi_parts(2)
            half = group(2)
            latent(0, tile_ps(half, 0), None)
            latent(1, tile_ps(half, 1), half)
            half = group()
            act.activation(va[:, :, :].rearrange("q t n -> q (t n)"), bank(4 * half, 2), ACT.Copy).then_inc(
                psum_free[half], 1)
            hi_parts(2)
            half = group(2)
            latent(2, tile_ps(half, 0), None)
            latent(3, tile_ps(half, 1), half)
            hi_parts(2)
            half = group(2)
            latent(4, tile_ps(half, 0), half)
            half = group()
            act.activation(rms_c[:, 0, :], tile_ps(half, 0), ACT.Sqrt, bias=eps_c, scale=1.0 / QL)
            act.activation(rms_c[:, 1, :], tile_ps(half, 1), ACT.Sqrt, bias=eps_c, scale=1.0 / KVL).then_inc(
                psum_free[half], 1)
            act.wait_ge(c_sum, 3)
            with act.Fori(0, GATES_N) as i:
                at_.loop(i, 4, 2)
                ahead.loop(i, 4)
                for j in range(2):
                    hi_parts(2)
                    half, done, _, free = at_.group(2)
                    complete(act, done)
                    for t in range(2):
                        n = 2 * j + t
                        gate = act.activation(stage[:, :], tile_ps(half, t), ACT.Sigmoid)
                        if t == 0:
                            gate.then_inc(gate_ready, 1)
                            act.wait_ge(gate_ready, i * 2 + (j + 1))
                        else:
                            gate.then_inc(psum_free[half], 1)
                            freed(act, half, free)
                        act.dma_start(gates_d[bass.ds(i * 4 + n, 1)].rearrange("a q n -> q (a n)"),
                                      stage[:, :]).then_inc(gate_saved, 16)
                        act.wait_ge(gate_saved, i * 64 + 16 * (n + 1))
                at_.end(GATES_N)
                ahead.end(GATES_N)
            hi_parts(2)
            half = group(2)
            act.activation(kr[lo:hi, :], tile_ps(half, 0)[lo:hi, :], ACT.Copy)
            act.wait_ge(q_norm_turned, 1)
            act.activation(q_norm, tile_ps(half, 1)[:, 0:TT], ACT.Copy, scale=SCALE_B).then_inc(psum_free[half], 1)

            def values(g):
                half = group()
                for j in range(2):
                    hd = 2 * g + j
                    last = act.activation(vb[:, :, hd * HEAD_DIM:(hd + 1) * HEAD_DIM],
                                          bank(4 * half + j).rearrange("q (t n) -> q t n", t=TT), ACT.Copy)
                last.then_inc(psum_free[half], 1)

            for kind, g in LATENT_HEADS:
                if kind == "vt":
                    values(g)
                    continue
                hi_parts(1)
                half = group(1)
                for j in range(2):
                    r, dst = (P, kvb) if kind == "kv" else (QB_DIM, qb)
                    last = act.activation(dst[0:r, 2 * g + j, :], tile_ps(half, j)[0:r, :], ACT.Copy)
                last.then_inc(psum_free[half], 1)

            def copy_probs(n):
                part = copied(n)[1]
                if part:
                    act.wait_ge(pt_ready, n + 1)
                    if n >= 2:
                        act.wait_ge(pv_done, n - 1)
                    r = slice(part[0] * P, part[1] * P)
                    act.activation(prob_t[:, n % 2, r], bank(4, 2)[:, r], ACT.Copy).then_inc(pt_act, 1)

            def y_hi(ti):
                dst = (yb_hi, ya_hi)[ti // TT]
                t = ti % TT
                act.wait_ge(y_ready, ti + 1)
                act.activation(dst[:, :, t * P:(t + 1) * P], y_f32[:, ti % 2, :].rearrange("q (k n) -> q k n", k=YT),
                               ACT.Copy).then_inc(y_hi_done, 1)

            for n, (br, i, hd) in enumerate(STEPS):
                ti = n // HEADS
                if n >= 2:
                    copy_probs(n - 2)
                act.wait_ge(shift_ready, n + 1)
                if n >= 2:
                    act.wait_ge(pt_ready, n - 1)
                e = KEYS[i]
                src = bank(2 * (n % 2), 2)[:, 0:e] if br == "B" else prob[:, n % 2, 0:e]
                k = (ti % 2) * HEADS + hd
                act.activation(prob[:, n % 2, 0:e], src, ACT.Exp, bias=shift_c[:, n % 4:n % 4 + 1],
                               scale=q_norm[:, i:i + 1] if br == "B" else SLOPES[hd],
                               accum_out=sums[:, k:k + 1]).then_inc(prob_ready, 1)
                if hd == 4 and ti >= 1:
                    y_hi(ti - 1)
            copy_probs(N - 2)
            copy_probs(N - 1)
            y_hi(2 * TT - 1)

            with act.Fori(0, DT // 2) as i:
                at_.loop(i, 2, 2)
                ahead.loop(i, 2)
                hi_parts(2)
                act.wait_ge(gated_ready, i + 1)
                act.activation(merged_hi[:, bass.ds(i * 2, 2), :].rearrange("q a n -> q (a n)"),
                               gated[:, :, :].rearrange("q a n -> q (a n)"), ACT.Copy).then_inc(m_hi_done, 1)
                at_.group(1)
                at_.group(1)
                at_.end(DT // 2)
                ahead.end(DT // 2)
            with act.Fori(0, OUT_N) as i:
                at_.loop(i, 4, 2, 2)
                ahead.loop(i, 4)
                for j in range(2):
                    hi_parts(2)
                    half, _, _, free = at_.group(2, turn=True)
                    freed(act, half, free)
                    act.activation(gated[:, :, :], h[:, bass.ds(i * 4 + 2 * j, 2), :], ACT.Square).then_inc(h_sq, 1)
                    act.wait_ge(sq_ready, i * 2 + (j + 2))
                at_.end(OUT_N)
                ahead.end(OUT_N)

            def root(count):
                half = group()
                act.activation(rms[:, :], tile_ps(half, 0), ACT.Sqrt, bias=eps_c, scale=1.0 / D).then_inc(rms_std, 1)

            def norm_hi_parts(gain):
                for k in range(DT):
                    act.activation(n_hi[:, k, :], h[:, k, :], ACT.Copy, scale=gain[:, k:k + 1]).then_inc(norm_hi, 1)

            root(0)
            norm_hi_parts(g_mlp_c)
            with act.Fori(0, FFN) as i:
                at_.loop(i, 8, 6)
                ahead.loop(i, 8)
                for j in range(2):
                    hi_parts(2)
                    half, _, _, free = at_.group(2)
                    for t in range(2):
                        n = 2 * j + t
                        if t == 0:
                            act.wait_ge(relu_ready, i * 2 + (j + 1))
                        else:
                            freed(act, half, free)
                        act.activation(tmp[:, j, t, :], tmp[:, j, t, :], ACT.Square).then_inc(hid_sq, 1)
                        act.wait_ge(hid_sq, i * 4 + (n + 1))
                        act.activation(hid_hi[:, n, :], tmp[:, j, t, :], ACT.Copy).then_inc(hid_hi_done, 1)
                for q in range(4):
                    hi_parts(1)
                    at_.group(1)
                at_.end(FFN)
                ahead.end(FFN)
            half = group()
            act.activation(pt_hi[:, :, :].rearrange("q a n -> q (a n)"), bank(4 * half, 4), ACT.Copy).then_inc(
                pt_hi_done, 1)
            freed(act, (PT_GROUP - 1) % 2, free_count(PT_GROUP - 1))
            norm_hi_parts(g_ple_c)
            for k in range(DT):
                if k >= 2:
                    act.wait_ge(sq_ready, SQ3 + k - 1)
                act.activation(tmp[:, 1, k % 2, :], h[:, k, :], ACT.Square).then_inc(h_sq, 1)
            for q in range(2 * OUT_N):
                hi_parts(2 if q < 3 else 1)
                half, _, _, free = at_.group(2)
                if q == 0:
                    root(1)
                act.wait_ge(gate_in, q + 1)
                freed(act, half, free)
                act.activation(tmp[:, q % 2, :, :], tmp[:, q % 2, :, :], ACT.Sigmoid).then_inc(gate_fn, 1)
                at_.group(1)
                if q < 3:
                    hi_parts(1)
            for t in range(TT):
                half = group()
                if t >= 2:
                    freed(act, half, free_count(FIN_GROUP + t - 2))
                act.activation(tmp[:, t % 2, 1, :], bank(4 * half, 2), ACT.Square,
                               accum_out=ss_c[:, t % 2:t % 2 + 1]).then_inc(fin_ss, 1)
                act.wait_ge(fin_ss, t + 1)
                act.activation(rstd_c[:, t % 2:t % 2 + 1], ss_c[:, t % 2:t % 2 + 1], ACT.Sqrt,
                               bias=eps_c, scale=1.0 / D).then_inc(fin_std, 1)

        @block.vector
        def _(dve):
            at_ = Place()
            steps = [0]

            def link(ins):
                steps[0] += 1
                ins.then_inc(dve_step, 1)
                dve.wait_ge(dve_step, steps[0])

            def group(slabs=0, turn=False):
                half, done, _, free = at_.group(slabs, turn)
                complete(dve, done)
                return half

            dve.memset(eps_c, EPS).then_inc(row_ready, 1)
            link(dve.memset(rows[0:1, :, :], 0.0))
            half_rope = ROPE // 2
            for j in range(half_rope):
                dve.memset(rows[0:1, 0, NOPE + j:NOPE + j + half_rope + 1:half_rope], THETA ** (-j / half_rope))
            dve.memset(rows[0:1, 1, NOPE:NOPE + half_rope], -1.0)
            dve.memset(rows[0:1, 1, NOPE + half_rope:QB_DIM], 1.0).then_inc(row_ready, 1)
            for t in range(YT):
                for j in range(2):
                    dve.memset(q_scale[j * HEAD_DIM:(j + 1) * HEAD_DIM, t:t + 1], SCALE_A / SLOPES[2 * t + j])

            def x_lo(t):
                half, _, _, _ = at_.group()
                dve.wait_ge(n_hi_done, t + 1)
                dve.tensor_tensor(n_lo[:, :, t * P:(t + 1) * P],
                                  bank(4 * half, 2).rearrange("q (k n) -> q k n", k=DT),
                                  n_hi[:, :, t * P:(t + 1) * P].bitcast(F32), ALU.subtract).then_inc(psum_free[half], 1)

            dve.wait_ge(gains_loaded, 16)
            for t in range(TT):
                dve.wait_ge(row_std, t + 1)
                r = rstd_c[:, t % 2:t % 2 + 1]
                link(dve.reciprocal(r, r))
                dve.scalar_tensor_tensor(x_tok[:, t, :], x_tok[:, t, :], r, gmix_row[:, :], ALU.mult,
                                         ALU.mult).then_inc(x_scaled, 1)
                if t >= 1:
                    x_lo(t - 1)
            x_lo(TT - 1)

            dve.wait_ge(pos_loaded, 16)
            dve.wait_ge(const_cols, 16 * 5)
            link(dve.tensor_copy(pos_f[:, :], pos_i[:, :]))
            dve.wait_ge(x_scaled, TT)
            link(dve.tensor_scalar(neg_pos, pos_ci[:, :], -1.0, None, ALU.mult))

            def distances(i):
                d = sc[:, SC_AT[i]:SC_AT[i] + KEYS[i]]
                link(dve.tensor_scalar(d, pos_f[:, 0:KEYS[i]], neg_pos[:, i:i + 1], None, ALU.add))
                return dve.scalar_tensor_tensor(d, d, -1.0, d, ALU.mult, ALU.max)

            for i in range(SELECT_FROM):
                distances(i).then_inc(near_dist, 1)
            dve.wait_ge(col_done, 1)
            link(dve.tensor_copy(inv_c[0:QB_DIM, :], bank(2)[0:QB_DIM, 0:2]))
            lo, hi = NOPE, QB_DIM
            ang, turns = rope_a[lo:hi, :], rope_k[lo:hi, :]
            link(dve.tensor_scalar(ang, pos_f[lo:hi, :], inv_c[lo:hi, 0:1], None, ALU.mult))
            for arg, quarter in ((rope_r[lo:hi, :], 0.25), (stage[lo:hi, :], 0.0)):
                link(dve.tensor_scalar(turns, ang, 0.15915494309189535, quarter, ALU.mult, ALU.add))
                link(dve.tensor_scalar(turns, turns, ROUND_MAGIC, None, ALU.add))
                link(dve.tensor_scalar(turns, turns, -ROUND_MAGIC, None, ALU.add))
                link(dve.scalar_tensor_tensor(arg, turns, -TWO_PI_1, ang, ALU.mult, ALU.add))
                link(dve.scalar_tensor_tensor(arg, turns, -TWO_PI_2, arg, ALU.mult, ALU.add))
                link(dve.scalar_tensor_tensor(arg, turns, -TWO_PI_3, arg, ALU.mult, ALU.add))
                link(dve.tensor_scalar(arg, arg, quarter * 2 * 3.141592653589793, PI, ALU.add, ALU.min))
                dve.tensor_scalar(arg, arg, -PI, None, ALU.max).then_inc(rope_arg, 1)
            for slabs in [2] * 6 + [0] + [2] * 2 + [0] + [2] * (2 * GATES_N + 1):
                at_.group(slabs)
            assert at_.groups == KR_GROUP + 1

            dve.wait_ge(wi_done, 1)
            dve.tensor_scalar(w_tok[:, :, :].rearrange("q t h -> q (t h)"), bank(7)[:, 0:TT * IDX_HEADS],
                              (IDX_HEADS * HEAD_DIM) ** -0.5, None, ALU.mult).then_inc(wi_copied, 1)
            dve.wait_ge(wi_copied, 1)
            m = 0
            for i in range(SELECT_FROM, TT):
                s_i = sc[:, SC_AT[i]:SC_AT[i] + KEYS[i]]
                for hd in range(IDX_HEADS):
                    dve.wait_ge(rel_done, m + 1)
                    if hd == 0:
                        ins = dve.tensor_scalar(s_i, rel[:, m % 2, 0:KEYS[i]], w_tok[:, i, hd:hd + 1], None, ALU.mult)
                    else:
                        dve.wait_ge(rel_used, m)
                        ins = dve.scalar_tensor_tensor(s_i, rel[:, m % 2, 0:KEYS[i]], w_tok[:, i, hd:hd + 1], s_i,
                                                       ALU.mult, ALU.add)
                    ins.then_inc(rel_used, 1)
                    m += 1

            dve.wait_ge(rope_saved, 32)
            for i in range(SELECT_FROM, TT):
                if i == TT - 1:
                    freed(dve, SUM_GROUP % 2, free_count(SUM_GROUP))
                    dve.reciprocal(rms_c[:, :, :], rms_c[:, :, :]).then_inc(latent_inv, 1)
                e = KEYS[i]
                s_i, work, eq, rank = sc[:, SC_AT[i]:SC_AT[i] + e], tk_work[:, 0:e], tk_eq[:, 0:e], tk_rank[:, 0:e]
                dve.wait_ge(far_masked, i - SELECT_FROM + 1)
                left = s_i
                for r in range(TOPK // 8):
                    link(dve.max(top8, left))
                    if r < TOPK // 8 - 1:
                        link(dve.match_replace(work, top8, left, LOWEST))
                        left = work
                bar = top8[:, 7:8]
                link(dve.tensor_scalar(work, s_i, bar, None, ALU.is_gt, ALU.add, accum_out=need_c))
                link(dve.tensor_scalar(need_c, need_c, -1.0, float(TOPK), ALU.mult, ALU.add))
                link(dve.tensor_scalar(eq, s_i, bar, None, ALU.is_equal))
                link(dve.tensor_tensor_scan(rank, eq, eq, 0.0, ALU.add, ALU.max))
                link(dve.scalar_tensor_tensor(eq, rank, need_c, eq, ALU.is_le, ALU.mult))
                link(dve.tensor_tensor(work, work, eq, ALU.add))
                link(dve.tensor_scalar(work, work, 0.0, -NEG, ALU.is_equal, ALU.mult))
                link(distances(i))
                dve.tensor_tensor(s_i, s_i, work, ALU.add).then_inc(dist_ready, 1)

            for kind, g in LATENT_HEADS:
                at_.group(0 if kind == "vt" else 1)
            dve.wait_ge(table_loaded, 32)
            for n in range(POOL_ROPES, HEADS + 1):
                rope(dve, n)

            def copy_probs(n):
                part = copied(n)[0]
                if part:
                    dve.wait_ge(pt_ready, n + 1)
                    if n >= 2:
                        dve.wait_ge(pv_done, n - 1)
                    r = slice(part[0] * P, part[1] * P)
                    dve.tensor_copy(prob_t[:, n % 2, r], bank(4, 2)[:, r]).then_inc(pt_dve, 1)

            def y_factors(ti):
                k = (ti % 2) * HEADS
                dve.wait_ge(prob_ready, HEADS * (ti + 1))
                link(dve.reciprocal(inv_sum, sums[:, k:k + HEADS]))
                dve.tensor_copy(y_f32[:, ti % 2, :].rearrange("q (h d) -> q h d", h=HEADS),
                                inv_sum.unsqueeze(2).to_broadcast([P, HEADS, HEAD_DIM])).then_inc(y_factor_ready, 1)

            def y_out(ti):
                dve.wait_ge(yt_ready, ti + 1)
                link(dve.tensor_copy(y_f32[:, ti % 2, :], bank(7)))
                dve.wait_ge(pv_done, HEADS * (ti + 1))
                dve.tensor_tensor(y_f32[:, ti % 2, :], bank(6), y_f32[:, ti % 2, :], ALU.mult).then_inc(y_ready, 1)

            def y_lo(ti):
                t = ti % TT
                r = slice(t * P, (t + 1) * P)
                dve.wait_ge(y_hi_done, ti + 1)
                dve.tensor_tensor((yb_lo, ya_lo)[ti // TT][:, :, r],
                                  y_f32[:, ti % 2, :].rearrange("q (k n) -> q k n", k=YT),
                                  (yb_hi, ya_hi)[ti // TT][:, :, r].bitcast(F32), ALU.subtract).then_inc(y_split, 1)

            for n, (br, i, hd) in enumerate(STEPS):
                ti = n // HEADS
                e = KEYS[i]
                top, shift = max_c[:, n % 4:n % 4 + 1], shift_c[:, n % 4:n % 4 + 1]
                if br == "A":
                    copy_probs(n - 2)
                dve.wait_ge(s_ready, n + 1)
                if br == "B":
                    link(dve.tensor_reduce(top, bank(2 * (n % 2), 2)[:, 0:e], AXIS.X, ALU.max))
                    dve.tensor_scalar(shift, top, q_norm[:, i:i + 1], -1.0, ALU.mult,
                                      ALU.mult).then_inc(shift_ready, 1)
                else:
                    dve.wait_ge(pt_ready, n - 1)
                    if n == HEADS * TT:
                        dve.wait_ge(near_masked, SELECT_FROM)
                    link(dve.tensor_tensor_reduce(prob[:, n % 2, 0:e], bank(2 * (n % 2), 2)[:, 0:e],
                                                  sc[:, SC_AT[i]:SC_AT[i] + e], 1.0, LOWEST, ALU.subtract, ALU.max,
                                                  top))
                    dve.tensor_scalar(shift, top, -SLOPES[hd], None, ALU.mult).then_inc(shift_ready, 1)
                if hd == 2 and ti >= 1:
                    y_out(ti - 1)
                if br == "B" and n >= 2:
                    copy_probs(n - 2)
                if hd == 1 and ti >= 1:
                    y_factors(ti - 1)
                if hd == 5 and ti >= 1:
                    y_lo(ti - 1)
            copy_probs(N - 2)
            copy_probs(N - 1)
            y_factors(2 * TT - 1)
            y_out(2 * TT - 1)
            y_lo(2 * TT - 1)

            with dve.Fori(0, DT // 2) as i:
                at_.loop(i, 2, 2)
                both = gated[:, :, :].rearrange("q a n -> q (a n)")
                siga, sigb = (sig_ab[:, b, :, :].rearrange("q a n -> q (a n)") for b in range(2))
                half = group(1)
                dve.wait_ge(sig_loaded, i * 32 + 32)
                dve.tensor_tensor(both, bank(4 * half, 4), siga, ALU.mult).then_inc(psum_free[half], 1)
                half, done, _, free = at_.group(1)
                complete(dve, done)
                dve.tensor_tensor(sigb, bank(4 * half, 4), sigb, ALU.mult).then_inc(psum_free[half], 1)
                freed(dve, half, free)
                dve.tensor_tensor(both, both, sigb, ALU.add).then_inc(gated_ready, 1)
                dve.wait_ge(m_hi_done, i + 1)
                dve.tensor_tensor(merged_lo[:, bass.ds(i * 2, 2), :].rearrange("q a n -> q (a n)"), both,
                                  merged_hi[:, bass.ds(i * 2, 2), :].rearrange("q a n -> q (a n)").bitcast(F32),
                                  ALU.subtract).then_inc(m_lo_done, 1)
                dve.wait_ge(m_lo_done, i + 1)
                at_.end(DT // 2)
            dve.memset(sq_sum[:, :], 0.0).then_inc(sq_ready, 1)
            with dve.Fori(0, OUT_N) as i:
                at_.loop(i, 4, 2, 2)
                for j in range(2):
                    half = group(2, turn=True)
                    dve.tensor_copy(h[:, bass.ds(i * 4 + 2 * j, 2), :].rearrange("q a n -> q (a n)"),
                                    bank(4 * half, 4)).then_inc(psum_free[half], 1)
                    dve.wait_ge(h_sq, i * 2 + (j + 1))
                    dve.tensor_tensor(gated[:, 0, :], gated[:, 0, :], gated[:, 1, :], ALU.add).then_inc(sq_pair, 1)
                    dve.wait_ge(sq_pair, i * 2 + (j + 1))
                    dve.wait_ge(sq_ready, i * 2 + (j + 1))
                    dve.tensor_tensor(sq_sum[:, :], sq_sum[:, :], gated[:, 0, :], ALU.add).then_inc(sq_ready, 1)
                at_.end(OUT_N)

            def inverse(count):
                at_.group()
                dve.wait_ge(rms_std, count + 1)
                dve.reciprocal(rms[:, :], rms[:, :]).then_inc(psum_free[(at_.groups - 1) % 2], 1)
                freed(dve, (at_.groups - 1) % 2, (at_.groups - 1) // 2 + 1)

            def norm_lo_parts(gain, before):
                for k in range(DT):
                    dve.wait_ge(norm_hi, before + k + 1)
                    dve.scalar_tensor_tensor(n_lo[:, k, :], h[:, k, :], gain[:, k:k + 1],
                                             n_hi[:, k, :].bitcast(F32), ALU.mult, ALU.subtract).then_inc(norm_lo, 1)

            inverse(0)
            norm_lo_parts(g_mlp_c, 0)
            with dve.Fori(0, FFN) as i:
                at_.loop(i, 8, 6)
                for j in range(2):
                    half = group(2)
                    for t in range(2):
                        dve.scalar_tensor_tensor(tmp[:, j, t, :], tile_ps(half, t), 0.0, rms[:, :], ALU.max,
                                                 ALU.mult).then_inc(relu_ready if t == 0 else psum_free[half], 1)
                    for t in range(2):
                        n = 2 * j + t
                        dve.wait_ge(hid_hi_done, i * 4 + (n + 1))
                        dve.tensor_tensor(hid_lo[:, n, :], tmp[:, j, t, :], hid_hi[:, n, :].bitcast(F32),
                                          ALU.subtract).then_inc(hid_lo_done, 1)
                for q in range(4):
                    half = group(1)
                    pair = h[:, 2 * q:2 * q + 2, :].rearrange("q a n -> q (a n)")
                    dve.tensor_tensor(pair, pair, bank(4 * half, 4), ALU.add).then_inc(psum_free[half], 1)
                at_.end(FFN)
            half, _, _, _ = at_.group()
            dve.wait_ge(pt_hi_done, 1)
            dve.tensor_tensor(pt_lo[:, :, :].rearrange("q a n -> q (a n)"), bank(4 * half, 4),
                              pt_hi[:, :, :].rearrange("q a n -> q (a n)").bitcast(F32),
                              ALU.subtract).then_inc(psum_free[half], 1)
            norm_lo_parts(g_ple_c, DT)
            for k in range(DT):
                dve.wait_ge(h_sq, 4 + k + 1)
                if k >= 1:
                    dve.wait_ge(sq_ready, SQ3 + k)
                    dve.tensor_tensor(sq_sum[:, :], sq_sum[:, :], tmp[:, 1, k % 2, :], ALU.add).then_inc(sq_ready, 1)
                else:
                    dve.tensor_copy(sq_sum[:, :], tmp[:, 1, k % 2, :]).then_inc(sq_ready, 1)
            for q in range(2 * OUT_N):
                half, done, _, free = at_.group(2)
                if q == 0:
                    inverse(1)
                complete(dve, done)
                for t in range(2):
                    dve.tensor_tensor(tmp[:, q % 2, t, :], tile_ps(half, t), rms[:, :], ALU.mult).then_inc(
                        gate_in if t == 0 else psum_free[half], 1)
                half = group(1)
                gate = tmp[:, q % 2, :, :].rearrange("q a n -> q (a n)")
                pair = h[:, 2 * q:2 * q + 2, :].rearrange("q a n -> q (a n)")
                dve.wait_ge(gate_fn, q + 1)
                dve.tensor_tensor(gate, gate, bank(4 * half, 4), ALU.mult).then_inc(psum_free[half], 1)
                freed(dve, half, free_count(at_.groups - 1))
                dve.tensor_tensor(pair, pair, gate, ALU.add).then_inc(h_final, 1)
            dve.wait_ge(gfin_loaded, 16)
            for t in range(TT):
                half, _, _, _ = at_.group()
                r = rstd_c[:, t % 2:t % 2 + 1]
                dve.wait_ge(fin_std, t + 1)
                link(dve.reciprocal(r, r))
                if t >= 2:
                    dve.wait_ge(stored[t % 2], 16 * (t // 2))
                dve.scalar_tensor_tensor(tmp[:, t % 2, 0, :], bank(4 * half, 2), r, gfin_row[:, :], ALU.mult,
                                         ALU.mult).then_inc(psum_free[half], 1)

        @block.tensor
        def _(pe):
            at_ = Place()

            def group():
                half, _, before, _ = at_.group()
                freed(pe, half, before)
                return half

            def product(half, tiles, slabs, moving, k_of=None, open_=False, first_wait=None):
                total = sum(nk for nk in slabs)
                k = 0
                for nk in slabs:
                    s, _, num, _ = at_.slab()
                    pe.wait_ge(lo_ready, num + 1)
                    for kk in range(nk):
                        if first_wait:
                            first_wait(k)
                        xh, xl = moving(k)
                        for j, (c, w) in enumerate(tiles):
                            wh, wl = w_hi[s][:, kk, c:c + w], w_lo[s][:, kk, c:c + w]
                            for wm, xm, a, z in ((wh, xh, True, False), (wh, xl, False, False), (wl, xh, False, True)):
                                for t in range(2):
                                    last = pe.matmul(bank(4 * half + 2 * j + t)[0:w, :], wm,
                                                     xm[:, t * HALF:(t + 1) * HALF],
                                                     start=(k == 0 and a), stop=(k == total - 1 and z and not open_))
                        k += 1
                    last.then_inc(slab_used, 1)

            FULL = ((0, P), (P, P))
            normed = lambda k: (n_hi[:, k, :], n_lo[:, k, :])

            def project(tiles=FULL, wait=None):
                half = group()
                product(half, tiles, (KT, KT), normed, first_wait=wait)

            pe.wait_ge(consts_ready, 4)
            pe.wait_ge(row_ready, 2)
            for c in range(2):
                last = pe.matmul(bank(2)[0:QB_DIM, c:c + 1], rows[0:1, c, 0:QB_DIM], ones[0:1, 0:1],
                                 start=True, stop=True)
            last.then_inc(col_done, 1)
            for t in range(TT):
                half = group()
                pe.wait_ge(x_scaled, t + 1)
                for k in range(DT):
                    last = pe.transpose(bank(4 * half, 2)[:, k * P:(k + 1) * P], x_tok[:, t, k * P:(k + 1) * P],
                                        ident[:, :])
                last.then_inc(turn_done, 1)
            freed(pe, (TT - 1) % 2, TT // 2)
            pe.wait_ge(rope_arg, 1)
            project()
            project(((0, HEAD_DIM + IDX_HEADS),))
            for half in range(2):
                freed(pe, half, at_.groups // 2)
            for t in range(TT):
                last = pe.transpose(bank(7)[:, t * IDX_HEADS:(t + 1) * IDX_HEADS],
                                    ki_wi[HEAD_DIM:HEAD_DIM + IDX_HEADS, t * P:(t + 1) * P],
                                    ident[HEAD_DIM:HEAD_DIM + IDX_HEADS, HEAD_DIM:HEAD_DIM + IDX_HEADS])
            last.then_inc(wi_done, 1)
            pe.wait_ge(ki_copied, 16)
            m = 0
            for i in range(SELECT_FROM, TT):
                for hd in range(IDX_HEADS):
                    if m == 3:
                        pe.wait_ge(wi_copied, 1)
                    if m >= 4:
                        pe.wait_ge(rel_done, m - 3)
                    r = slice((hd % 2) * HEAD_DIM, (hd % 2 + 1) * HEAD_DIM)
                    for c in range(0, KEYS[i], HALF):
                        e = min(HALF, KEYS[i] - c)
                        last = pe.matmul(bank(2 * (m % 4) + c // HALF)[:, 0:e], qi[r, hd // 2, i * P:(i + 1) * P],
                                         ki[r, c:c + e], start=True, stop=True)
                    last.then_inc(idx_done, 1)
                    m += 1
            pe.wait_ge(rel_done, m)
            for _ in range(4):
                project()
            half = group()
            freed(pe, VA_GROUP % 2, (VA_GROUP - 2) // 2 + 1)
            for t in range(TT):
                last = pe.transpose(bank(4 * half, 2)[:, t * P:(t + 1) * P], c32[:, t * P:(t + 1) * P], ident[:, :])
            last.then_inc(turn_done, 1)
            project()
            project(((0, P),))
            half = group()
            pe.wait_ge(c_sum, 3)
            pe.wait_ge(c_sq, QT + KVT)
            for c in range(2):
                for t in range(2):
                    last = pe.matmul(bank(4 * half + 2 * c + t), ones[:, :], rms_c[:, c, t * HALF:(t + 1) * HALF],
                                     start=True, stop=True)
            last.then_inc(turn_done, 1)
            with pe.Fori(0, GATES_N) as i:
                at_.loop(i, 4, 2, 2)
                project()
                project()
                at_.end(GATES_N)
            project(((0, QB_DIM),))
            pe.wait_ge(latent_inv, 1)
            for t in range(TT):
                last = pe.matmul(tile_ps((at_.groups - 1) % 2, 1)[:, t:t + 1], rms_c[0:1, 0, t * P:(t + 1) * P],
                                 ones[0:1, 0:1], start=True, stop=True)
            last.then_inc(q_norm_turned, 1)
            pe.wait_ge(c_lo, QT + KVT)
            for kind, g in LATENT_HEADS:
                half = group()
                if kind == "kv":
                    product(half, FULL, (KVT,), lambda k: (ckv_hi[:, k, :], ckv_lo[:, k, :]))
                elif kind == "q":
                    product(half, ((0, QB_DIM), (QB_DIM, QB_DIM)), (QT,),
                            lambda k: (cq_hi[:, k, :], cq_lo[:, k, :]))
                else:
                    pe.wait_ge(kv_scaled, g + 1)
                    for j in range(2):
                        for t in range(TT):
                            last = pe.transpose(bank(4 * half + j)[:, t * HEAD_DIM:(t + 1) * HEAD_DIM],
                                                kvb[HEAD_DIM:P, 2 * g + j, t * P:(t + 1) * P],
                                                ident[HEAD_DIM:P, HEAD_DIM:P])
                    last.then_inc(turn_done, 1)

            for half in range(2):
                freed(pe, half, (at_.groups + 1 - half) // 2)
            pe.wait_ge(kr_copied, 16 * HEADS)
            pe.wait_ge(rope_done[0], 3 * POOL_ROPES)
            pe.wait_ge(rope_done[1], 3 * (HEADS + 1 - POOL_ROPES))

            def scores(n):
                br, i, hd = STEPS[n]
                b = 2 * (n % 2)
                if n >= 2:
                    if STEPS[n - 2][0] == "B":
                        pe.wait_ge(prob_ready, n - 1)
                    else:
                        pe.wait_ge(shift_ready, n - 1)
                q = slice(i * P, (i + 1) * P)
                if br == "B":
                    lhs, rhs = qb[0:QB_DIM, hd, q], kvb[0:QB_DIM, hd, :]
                else:
                    r = slice((hd % 2) * HEAD_DIM, (hd % 2 + 1) * HEAD_DIM)
                    lhs, rhs = qa[r, hd // 2, q], ka[r, hd // (HEADS // KV_HEADS_A), :]
                for c in range(0, KEYS[i], HALF):
                    e = min(HALF, KEYS[i] - c)
                    final = c + e == KEYS[i]
                    last = pe.matmul(bank(b + c // HALF)[:, 0:e], lhs, rhs[:, c:c + e], start=True,
                                     stop=not (final and br == "B"))
                if br == "B":
                    last = pe.matmul(bank(b, 2)[:, i * P:(i + 1) * P], ident_b[:, :], causal_b[:, :],
                                     start=False, stop=True)
                last.then_inc(s_ready, 1)

            def turn_probs(n):
                br, i, hd = STEPS[n]
                pe.wait_ge(prob_ready, n + 1)
                if n >= 1:
                    pe.wait_ge(pt_dve, copies(0, n))
                    if copies(1, n):
                        pe.wait_ge(pt_act, copies(1, n))
                for k in range(i + 1):
                    last = pe.transpose(bank(4, 2)[:, k * P:(k + 1) * P], prob[:, n % 2, k * P:(k + 1) * P], ident[:, :])
                last.then_inc(pt_ready, 1)

            def sum_values(n):
                br, i, hd = STEPS[n]
                ti = n // HEADS
                pe.wait_ge(pt_dve, copies(0, n + 1))
                if copies(1, n + 1):
                    pe.wait_ge(pt_act, copies(1, n + 1))
                if hd == 0 and ti >= 1:
                    pe.wait_ge(y_ready, ti)
                c = hd // (HEADS // KV_HEADS_A)
                for k in range(i + 1):
                    v = vb[:, k, hd * HEAD_DIM:(hd + 1) * HEAD_DIM] if br == "B" else \
                        va[:, k, c * HEAD_DIM:(c + 1) * HEAD_DIM]
                    last = pe.matmul(bank(6)[(hd % 2) * HEAD_DIM:(hd % 2 + 1) * HEAD_DIM,
                                             hd // 2 * P:(hd // 2 + 1) * P],
                                     v, prob_t[:, n % 2, k * P:(k + 1) * P], start=(k == 0), stop=(k == i))
                last.then_inc(pv_done, 1)

            def turn_y(ti):
                pe.wait_ge(y_factor_ready, ti + 1)
                for k in range(YT):
                    last = pe.transpose(bank(7)[:, k * P:(k + 1) * P], y_f32[:, ti % 2, k * P:(k + 1) * P], ident[:, :])
                last.then_inc(yt_ready, 1)

            scores(0)
            for n, (br, i, hd) in enumerate(STEPS):
                if n + 1 < N:
                    scores(n + 1)
                if n >= 1:
                    turn_probs(n - 1)
                if n >= 2:
                    sum_values(n - 2)
                if hd == 1 and n >= HEADS:
                    turn_y(n // HEADS - 1)
            turn_probs(N - 1)
            sum_values(N - 2)
            sum_values(N - 1)
            turn_y(2 * TT - 1)

            pe.wait_ge(y_split, 2 * TT)
            with pe.Fori(0, DT // 2) as i:
                at_.loop(i, 2, 2, 2)
                for yh, yl in ((ya_hi, ya_lo), (yb_hi, yb_lo)):
                    half = group()
                    product(half, FULL, (KT,), lambda k: (yh[:, k, :], yl[:, k, :]))
                at_.end(DT // 2)
            pe.wait_ge(m_lo_done, DT // 2)
            with pe.Fori(0, OUT_N) as i:
                at_.loop(i, 4, 2, 2)
                for j in range(2):
                    half = group()
                    product(half, FULL, (KT, KT), lambda k: (merged_hi[:, k, :], merged_lo[:, k, :]), open_=True)
                    pe.wait_ge(xs_loaded[j], i * 16 + 16)
                    for c in range(2):
                        for t in range(TT):
                            last = pe.matmul(bank(4 * half + 2 * c, 2)[:, t * P:(t + 1) * P],
                                             xs[:, j, t, c * P:(c + 1) * P], ident[:, :], start=False,
                                             stop=(t % 4 == 3))
                    last.then_inc(turn_done, 1)
                at_.end(OUT_N)

            def square_sums():
                for t in range(2):
                    last = pe.matmul(bank(4 * half + t), ones[:, :], sq_sum[:, t * HALF:(t + 1) * HALF],
                                     start=True, stop=True)
                last.then_inc(turn_done, 1)

            half = group()
            pe.wait_ge(sq_ready, 2 * OUT_N + 1)
            square_sums()
            with pe.Fori(0, FFN) as i:
                at_.loop(i, 8, 6, 6)
                project(wait=lambda k: pe.wait_ge(norm_lo, k + 1))
                project()

                def hid_there(k):
                    pe.wait_ge(hid_lo_done, i * 4 + (k + 1))

                for q in range(4):
                    half = group()
                    product(half, FULL, (KT,), lambda k: (hid_hi[:, k, :], hid_lo[:, k, :]),
                            first_wait=hid_there if q == 0 else None)
                at_.end(FFN)
            half = group()
            pe.wait_ge(p_loaded, 16)
            for f in range(2):
                for t in range(TT):
                    last = pe.transpose(bank(4 * half + 2 * f, 2)[:, t * P:(t + 1) * P], p_tok[:, t, f * P:(f + 1) * P],
                                        ident[:, :])
            last.then_inc(turn_done, 1)
            for q in range(2 * OUT_N):
                project(wait=(lambda k: pe.wait_ge(norm_lo, DT + k + 1)) if q == 0 else None)
                if q == 0:
                    half = group()
                    pe.wait_ge(sq_ready, SQ3 + DT)
                    square_sums()
                half = group()
                if q == 0:
                    freed(pe, PT_GROUP % 2, free_count(PT_GROUP))
                product(half, FULL, (2,), lambda k: (pt_hi[:, k, :], pt_lo[:, k, :]))
            pe.wait_ge(h_final, 2 * OUT_N)
            for t in range(TT):
                half = group()
                for k in range(DT):
                    last = pe.transpose(bank(4 * half, 2)[:, k * P:(k + 1) * P], h[:, k, t * P:(t + 1) * P], ident[:, :])
                last.then_inc(turn_done, 1)


_INS = ['x', 'p', 'positions', 'g_mix', 'w_in', 'g_cq', 'w_uq', 'g_ckv', 'w_ukv', 'w_pa', 'w_pb', 'w_out', 'g_mlp',
        'w_ff1', 'w_ff2', 'g_ple', 'w_ple_gate', 'w_ple', 'g_final']


def kernel(**inputs):
    import numpy as _np
    import concourse.bacc as _bacc
    from concourse import mybir as _mybir
    from concourse.bass_utils import run_bass_kernel_spmd as _run

    nc = _bacc.Bacc("TRN2", target_bir_lowering=False, num_devices=1)
    arrays, args = {}, []
    for name in _INS:
        a = _np.ascontiguousarray(inputs[name])
        arrays[f"in_{name}_dram"] = a
        args.append(nc.dram_tensor(f"in_{name}_dram", a.shape, _mybir.dt.from_np(a.dtype), kind="ExternalInput").ap())
    args.append(nc.dram_tensor("out_0_dram", inputs["x"].shape, _mybir.dt.float32, kind="ExternalOutput").ap())
    build(nc, *args)
    r = _run(nc, [arrays], core_ids=[0])
    return r.results[0]["out_0_dram"]
```

```python
from contextlib import ExitStack

import concourse.bass as bass
from concourse import mybir

P = 128
F32 = mybir.dt.float32
F32R = mybir.dt.float32r
BF16 = mybir.dt.bfloat16
I32 = mybir.dt.int32
ALU = mybir.AluOpType
ACT = mybir.ActivationFunctionType
AXIS = mybir.AxisListType

HEADS, HEAD_DIM = 8, 64
KV_HEADS_A = 2
IDX_HEADS = 4
TOPK = 256
NOPE, ROPE = 64, 32
THETA = 10000.0
EPS = 1e-6
NEG = -1e30
LOWEST = -3e38
SCALE_A = HEAD_DIM ** -0.5
SCALE_B = (NOPE + ROPE) ** -0.5
ROUND_MAGIC = 1.5 * 2 ** 23
TWO_PI_1 = 6.28125
TWO_PI_2 = 0.0019350051879882812
TWO_PI_3 = 3.019916050561733e-07
PI = 3.1415925
KT, WCOL = 4, 256


class Place:

    def __init__(self):
        self.slabs = self.groups = self.turns = 0
        self.i, self.per = None, (0, 0, 0)

    def loop(self, i, slabs=0, groups=0, turns=0):
        assert slabs % 2 == 0 and groups % 2 == 0
        self.i, self.per = i, (slabs, groups, turns)
        self.start = (self.slabs, self.groups, self.turns)

    def end(self, trips):
        now = (self.slabs, self.groups, self.turns)
        assert tuple(n - s for n, s in zip(now, self.start)) == self.per, (now, self.start, self.per)
        self.slabs, self.groups, self.turns = (n + p * (trips - 1) for n, p in zip(now, self.per))
        self.i, self.per = None, (0, 0, 0)

    def value(self, first, per):
        return first if self.i is None or per == 0 else self.i * per + first

    def slab(self):
        n, per = self.slabs, self.per[0]
        self.slabs += 1
        return n % 2, n, self.value(n, per), self.value(16 * (n // 2 + 1), 8 * per)

    def group(self, slabs=0, turn=False):
        n, per = self.groups, self.per[1]
        self.groups += 1
        self.slabs += slabs
        if turn or not slabs:
            self.turns += 1
            done = ("turn", self.value(self.turns, self.per[2]))
        else:
            done = ("slab", self.value(self.slabs, self.per[0]))
        return n % 2, done, self.value(n // 2, per // 2), self.value(n // 2 + 1, per // 2)


def build(nc, x, p, positions, g_mix, w_in, g_cq, w_uq, g_ckv, w_ukv, w_pa, w_pb, w_out, g_mlp, w_ff1, w_ff2,
          g_ple, w_ple_gate, w_ple, g_final, out):
    _, S, D = x.shape
    FF = w_ff1.shape[2]
    QL, KVL, PL = w_uq.shape[1], w_ukv.shape[1], w_ple.shape[1]
    TT = S // P
    DT = D // P
    QT, KVT = QL // P, KVL // P
    HALF = S // 2
    HD = HEADS * HEAD_DIM
    YT = HD // P
    QI0 = HD + 2 * KV_HEADS_A * HEAD_DIM
    KI0 = QI0 + IDX_HEADS * HEAD_DIM
    CQ0 = KI0 + HEAD_DIM + IDX_HEADS
    KR0 = CQ0 + QL + KVL
    G0 = KR0 + ROPE
    QB_DIM = NOPE + ROPE
    assert (S, D) == (1024, 1024) and QT == 3 and KVT == 2
    GATES_N = 2 * D // (2 * WCOL)
    OUT_N = D // (2 * WCOL)
    CHUNK = 4
    FFN = FF // (CHUNK * P)
    KEYS = [(i + 1) * P for i in range(TT)]
    SC_AT = [sum(KEYS[:i]) for i in range(TT)]
    SELECT_FROM = TOPK // P

    x2, p2, out2 = x[0], p[0, 0], out[0]
    wi, uq, ukv, pa, pb, wo = w_in[0], w_uq[0], w_ukv[0], w_pa[0], w_pb[0], w_out[0]
    f1, f2, pg, pw = w_ff1[0], w_ff2[0], w_ple_gate[0], w_ple[0]
    gates_d = nc.dram_tensor("gates_scratch", (2 * D // P, P, S), F32, kind="Internal").ap()
    rope_d = nc.dram_tensor("rope_scratch", (2, ROPE, S), F32, kind="Internal").ap()

    ctx = ExitStack()
    with ctx:
        K = 1024
        base = (nc.sbuf_base + 31) // 32 * 32

        def at(name, off, shape, dt=F32):
            return nc.alloc_sbuf_tensor_at(name, [P] + shape, dt, offset=base + off)

        W_AT, NX, R1, R2, T = 0, 24 * K, 88 * K, 136 * K, 182 * K
        MISC = 198 * K
        w_raw = [at(f"w_raw{s}", W_AT + s * 4 * K, [KT, WCOL]) for s in range(2)]
        w_hi = [at(f"w_hi{s}", W_AT + (8 + s * 4) * K, [KT, WCOL], F32R) for s in range(2)]
        w_lo = [at(f"w_lo{s}", W_AT + (16 + s * 4) * K, [KT, WCOL], F32R) for s in range(2)]
        n_hi, n_lo = at("n_hi", NX, [DT, S], F32R), at("n_lo", NX + 32 * K, [DT, S], F32R)
        qb, kvb = at("qb", NX, [HEADS, S]), at("kvb", NX + 32 * K, [HEADS, S])
        merged_hi = at("merged_hi", NX, [DT, S], F32R)
        n2_hi, n2_lo = at("n2_hi", NX + 32 * K, [DT, S], F32R), at("n2_lo", NX, [DT, S], F32R)
        ya_hi, ya_lo = at("ya_hi", NX + 32 * K, [YT, S], F32R), at("ya_lo", NX + 48 * K, [YT, S], F32R)
        x_tok = at("x_tok", R1, [TT, D])
        qi = at("qi", R1, [2, S])
        ki = at("ki", R1 + 8 * K, [S])
        ki_wi = at("ki_wi", R1 + 12 * K, [S])
        rel = at("rel", R1 + 16 * K, [2, S])
        ckv_hi, ckv_lo = at("ckv_hi", R1, [KVT, S], F32R), at("ckv_lo", R1 + 8 * K, [KVT, S], F32R)
        ckv, cq = at("ckv", R1 + 8 * K, [KVT, S]), at("cq", R1 + 28 * K, [QT, S])
        cq_hi, cq_lo = at("cq_hi", R1 + 16 * K, [QT, S], F32R), at("cq_lo", R1 + 28 * K, [QT, S], F32R)
        rms_c = at("rms_c", R1 + 40 * K, [2, S])
        vb = at("vb", R1, [TT, HD])
        yb_hi, yb_lo = at("yb_hi", R1 + 16 * K, [YT, S], F32R), at("yb_lo", R1 + 32 * K, [YT, S], F32R)
        yb = at("yb", R1 + 32 * K, [YT, S])
        h = at("h", R1, [DT, S])
        sc = at("sc", R2, [sum(KEYS)])
        qa = at("qa", R2 + 18 * K, [YT, S])
        ka = at("ka", R2 + 34 * K, [KV_HEADS_A, S])
        va = at("va", R2 + 42 * K, [TT, P])
        gmix_row = at("gmix_row", R2, [D])
        merged_lo = at("merged_lo", R2, [DT, S], F32R)
        gated = at("gated", R2 + 32 * K, [2, S])
        hid_hi, hid_lo = at("hid_hi", R2, [CHUNK, S], F32R), at("hid_lo", R2 + 16 * K, [CHUNK, S], F32R)
        p_tok = at("p_tok", R1 + 32 * K, [TT, PL])
        pt_hi, pt_lo = at("pt_hi", R2 + 32 * K, [2, S], F32R), at("pt_lo", R1 + 40 * K, [2, S], F32R)
        tk_early = [at(f"tk_early{b}", T + 4 * b * K, [S]) for b in range(3)]
        tk_late = [at(f"tk_late{b}", R1 + (16 + 4 * b) * K, [S]) for b in range(3)]
        stage = at("stage", T + 12 * K, [S])
        rope_a = at("rope_a", T, [S])
        rope_k = at("rope_k", T + 4 * K, [S])
        rope_r = at("rope_r", T + 8 * K, [S])
        rope_cos, rope_sin = at("rope_cos", T + 4 * K, [S]), at("rope_sin", T + 8 * K, [S])
        swap = [at("swap0", MISC + 4 * K, [S]), at("swap1", R1 + 40 * K, [S])]
        kr = at("kr", T + 12 * K, [S])
        prob = at("prob", T, [2, S])
        prob_t = at("prob_t", T + 8 * K, [2, S])
        sig_ab = at("sig_ab", T, [2, 2, S])
        xs = at("xs", T, [2, TT, WCOL])
        tmp = at("tmp", T, [2, 2, S])
        pos_f = at("pos_f", MISC, [S])
        rms = at("rms", MISC, [S])
        va_features = at("va_features", MISC + 4 * K, [S])
        y_f32 = at("y_f32", MISC + 4 * K, [2, HD])
        sq_sum = at("sq_sum", MISC + 4 * K, [S])
        gfin_row = at("gfin_row", MISC + 4 * K, [D])
        m = MISC + 8 * K
        ident = at("ident", m, [P])
        ones = at("ones", m + 512, [P])
        ident_b = at("ident_b", m + 1024, [P], BF16)
        causal_b = at("causal_b", m + 1280, [P], BF16)
        small = m + 1536
        COLS = 92
        assert base + small + 4 * COLS <= nc.sbuf_usable_end
        cols = at("cols", small, [COLS])
        names = {}

        def col(name, n=1):
            at0 = names.setdefault(name, (sum(v[1] for v in names.values()), n))[0]
            assert at0 + n <= COLS
            return cols[:, at0:at0 + n]

        g_cq_c, g_ckv_c = col("g_cq", QT), col("g_ckv", KVT)
        g_mlp_c, g_ple_c = col("g_mlp", DT), col("g_ple", DT)
        eps_c = col("eps")
        q_scale = col("q_scale", YT)
        inv_c = col("inv", 2)
        ss_c = col("ss", 2)
        rstd_c = col("rstd", 2)
        top8 = col("top8", 8)
        need_c = col("need")
        max_c = col("max", 4)
        shift_c = col("shift", 4)
        sums = col("sums", 2 * HEADS)
        inv_sum = col("inv_sum", HEADS)
        neg_pos = col("neg_pos", TT)
        q_norm = col("q_norm", TT)
        w_tok = at("w_tok", R1 + 32 * K, [TT, IDX_HEADS])
        pos_i = at("pos_i", R1 + 33 * K, [S], I32)
        pos_ci = at("pos_ci", R1 + 37 * K, [TT], I32)
        rows = at("rows", R1 + 38 * K, [2, P])

        ps = ctx.enter_context(nc.psum_tensor("ps", [P, 8, HALF], F32))

        def bank(b, n=1):
            return ps[:, b:b + n, :].rearrange("p b n -> p (b n)")

        def tile_ps(half, j, n=1):
            return bank(4 * half + 2 * j, 2 * n)

        def sem(name):
            return ctx.enter_context(nc.semaphore(name))

        raw_loaded = [sem("raw_loaded0"), sem("raw_loaded1")]
        hi_ready, lo_ready = sem("hi_ready"), sem("lo_ready")
        slab_used, turn_done = sem("slab_used"), sem("turn_done")
        psum_free = [sem("psum_free0"), sem("psum_free1")]
        x_loaded = [sem(f"x_loaded{t}") for t in range(DT)]
        xs_loaded = [sem("xs_loaded0"), sem("xs_loaded1")]
        stored = [sem("stored0"), sem("stored1")]
        const_cols = sem("const_cols")
        consts_half = sem("consts_half")
        consts_ready = sem("consts_ready")
        row_ready = sem("row_ready")
        gains_loaded = sem("gains_loaded")
        pos_loaded = sem("pos_loaded")
        row_ss = sem("row_ss")
        row_std = sem("row_std")
        x_scaled = sem("x_scaled")
        n_hi_done = sem("n_hi_done")
        col_done = sem("col_done")
        inv_copied = sem("inv_copied")
        rope_arg = sem("rope_arg")
        rope_saved = sem("rope_saved")
        idx_ready = sem("idx_ready")
        ki_copied = sem("ki_copied")
        wi_done = sem("wi_done")
        wi_copied = sem("wi_copied")
        idx_done = sem("idx_done")
        rel_done = sem("rel_done")
        rel_used = sem("rel_used")
        near_dist = sem("near_dist")
        sq_pair = sem("sq_pair")
        far_masked = sem("far_masked")
        near_masked = sem("near_masked")
        dist_ready = sem("dist_ready")
        ka_ready = sem("ka_ready")
        ka_copied = sem("ka_copied")
        c_scaled = sem("c_scaled")
        c_sq = sem("c_sq")
        c_hi = sem("c_hi")
        c_lo = sem("c_lo")
        c_sum = sem("c_sum")
        gate_ready = sem("gate_ready")
        gate_saved = sem("gate_saved")
        table_loaded = sem("table_loaded")
        swap_loaded = [sem("swap_loaded0"), sem("swap_loaded1")]
        rope_done = sem("rope_done")
        q_norm_turned = sem("q_norm_turned")
        kr_copied = sem("kr_copied")
        s_ready = sem("s_ready")
        shift_ready = sem("shift_ready")
        prob_ready = sem("prob_ready")
        pt_ready = sem("pt_ready")
        pt_dve = sem("pt_dve")
        pt_act = sem("pt_act")
        pv_done = sem("pv_done")
        y_factor_ready = sem("y_factor_ready")
        y_ready = sem("y_ready")
        yt_ready = sem("yt_ready")
        y_hi_done = sem("y_hi_done")
        y_split = sem("y_split")
        yb_hi_done = sem("yb_hi_done")
        yb_split = sem("yb_split")
        sig_loaded = sem("sig_loaded")
        gated_ready = sem("gated_ready")
        m_hi_done = sem("m_hi_done")
        m_lo_done = sem("m_lo_done")
        h_sq = sem("h_sq")
        sq_ready = sem("sq_ready")
        norm_hi = sem("norm_hi")
        norm_lo = sem("norm_lo")
        relu_ready = sem("relu_ready")
        hid_sq = sem("hid_sq")
        hid_hi_done = sem("hid_hi_done")
        hid_lo_done = sem("hid_lo_done")
        p_loaded = sem("p_loaded")
        pt_hi_done = sem("pt_hi_done")
        gate_in = sem("gate_in")
        gate_fn = sem("gate_fn")
        h_final = sem("h_final")
        gfin_loaded = sem("gfin_loaded")
        fin_ss = sem("fin_ss")
        fin_std = sem("fin_std")
        dve_step = sem("dve_step")
        act_step = sem("act_step")

        def complete(eng, done):
            eng.wait_ge(turn_done if done[0] == "turn" else slab_used, done[1])

        def freed(eng, half, count):
            if not isinstance(count, int) or count > 0:
                eng.wait_ge(psum_free[half], count)

        def wt(w, k0, nk, c0, n):
            return w[k0 * P:(k0 + nk) * P, :].rearrange("(k q) c -> q k c", q=P)[:, :, bass.ds(c0, n)]

        VA_GROUP = TT + 6
        SUM_GROUP = VA_GROUP + 3 + 2 * GATES_N
        KR_GROUP = SUM_GROUP + 1
        LATENT_HEADS = [(kind, g) for kind in ("q", "kv", "vt") for g in range(HEADS // 2)]
        KV_GROUP, UQ_GROUP, VT_GROUP = ([KR_GROUP + 1 + LATENT_HEADS.index((kind, g)) for g in range(HEADS // 2)]
                                        for kind in ("kv", "q", "vt"))
        OUT_GROUP = KR_GROUP + 1 + len(LATENT_HEADS) + DT
        RMS_GROUPS = (OUT_GROUP + 2 * OUT_N, OUT_GROUP + 2 * OUT_N + 2 + 6 * FFN)
        FIN_GROUP = RMS_GROUPS[1] + 1 + 4 * OUT_N
        SQ3 = 2 * OUT_N + 1
        IDX_ORDER = [hd for first in range(2) for hd in range(first, IDX_HEADS, 2)]
        SLOPES = [2.0 ** (-8.0 * (hd + 1) / HEADS) for hd in range(HEADS)]
        LATENTS = [(cq[:, k, :], cq_lo[:, k, :], cq_hi[:, k, :], rms_c[:, 0, :], k == 0, max(k - 1, 0), g_cq_c[:, k:k + 1])
                   for k in range(QT)]
        LATENTS += [(ckv[:, k, :], ckv_lo[:, k, :], ckv_hi[:, k, :], rms_c[:, 1, :], k == 0, QT - 1, g_ckv_c[:, k:k + 1])
                    for k in range(KVT)]

        def free_count(g):
            return g // 2 + 1

        ROPES = [kr] + [qb[:, hd, :] for hd in range(HEADS)]
        ROUNDS = 2 * (TOPK // 8) - 1
        PASSES = ROUNDS + 9

        STEPS = [(br, i, hd) for br in "BA" for i in range(TT) for hd in range(HEADS)]
        N = len(STEPS)
        BANK_BLOCKS = HALF // P

        def copied(n):
            _, i, hd = STEPS[n]
            if i >= BANK_BLOCKS:
                return (BANK_BLOCKS, i + 1), (0, BANK_BLOCKS)
            return ((0, i + 1), None) if hd % 2 == 0 and n not in LATE_STEPS else (None, (0, i + 1))

        def copies(engine, n):
            return sum(1 for k in range(n) if copied(k)[engine])

        B_HI_FROM = TT - YT
        LATE_STEPS = [n for n, (br, i, hd) in enumerate(STEPS)
                      if (br == "B" and i >= 2 and (i >= 3 or hd not in (1, 2))) or
                      (br == "A" and ((i == 1 and hd in (0, 3, 6, 7)) or (2 <= i < B_HI_FROM and hd not in (1, 2))))]
        AFTER_KEYS = 4
        LAST_EARLY = PASSES - len(LATE_STEPS) - 1 - AFTER_KEYS
        assert LAST_EARLY % 2 == 1

        block = ctx.enter_context(nc.Block())

        @block.sync
        def _(sp):
            at_ = Place()

            def load(src, nk=KT, n=WCOL):
                s, first, num, _ = at_.slab()
                if first >= 2:
                    sp.wait_ge(lo_ready, num - 1)
                sp.dma_start(w_raw[s][:, 0:nk, 0:n], src).then_inc(raw_loaded[s], 16)

            def load_kn(w, c0, n=WCOL):
                for k0 in (0, KT):
                    load(wt(w, k0, KT, c0, n), KT, n)

            sp.dma_start(x_tok[:, 0, :], x2[0:P, :]).then_inc(x_loaded[0], 16)
            sp.dma_start(gmix_row[:, :], g_mix[0].partition_broadcast(P)).then_inc(gains_loaded, 16)
            for t in range(1, TT):
                sp.dma_start(x_tok[:, t, :], x2[t * P:(t + 1) * P, :]).then_inc(x_loaded[t], 16)
            sp.dma_start(pos_i[:, :], positions[0].partition_broadcast(P)).then_inc(pos_loaded, 16)
            load_kn(wi, QI0)
            load_kn(wi, KI0, HEAD_DIM + IDX_HEADS)
            load_kn(wi, 0)
            sp.wait_ge(idx_ready, 1)
            sp.dma_start(ki[HEAD_DIM:P, :], ki[0:HEAD_DIM, :]).then_inc(ki_copied, 16)
            load_kn(wi, WCOL)
            load_kn(wi, HD)
            load_kn(wi, CQ0)
            sp.wait_ge(ka_ready, 2)
            sp.dma_start(ka[HEAD_DIM:P, 0, :], ka[0:HEAD_DIM, 0, :]).then_inc(ka_copied, 16)
            sp.dma_start(ka[0:HEAD_DIM, 1, :], ka[HEAD_DIM:P, 1, :]).then_inc(ka_copied, 16)
            load_kn(wi, CQ0 + WCOL)
            load_kn(wi, CQ0 + 2 * WCOL, P)
            with sp.Fori(0, GATES_N) as i:
                at_.loop(i, 4, 0)
                for j in range(2):
                    load_kn(wi, i * (2 * WCOL) + (G0 + j * WCOL))
                at_.end(GATES_N)
            load_kn(wi, KR0 - NOPE, QB_DIM)
            sp.wait_ge(rope_saved, 32)
            sp.wait_ge(dist_ready, TT - 1 - SELECT_FROM)
            lo, mid, hi = NOPE, NOPE + ROPE // 2, QB_DIM
            sp.dma_start(rope_cos[lo:hi, :], rope_d[0]).then_inc(table_loaded, 16)
            sp.dma_start(rope_sin[lo:hi, :], rope_d[1]).then_inc(table_loaded, 16)

            def swap_halves(n):
                if n >= 2:
                    sp.wait_ge(rope_done, n - 1)
                b = n % 2
                sp.dma_start(swap[b][lo:mid, :], ROPES[n][mid:hi, :]).then_inc(swap_loaded[b], 16)
                sp.dma_start(swap[b][mid:hi, :], ROPES[n][lo:mid, :]).then_inc(swap_loaded[b], 16)

            def load_kv(g):
                load(wt(ukv, 0, KVT, g * WCOL, WCOL), KVT)

            def load_q(g):
                load(wt(uq, 0, QT, g * 2 * QB_DIM, 2 * QB_DIM), QT, 2 * QB_DIM)

            load_q(0)
            load_q(1)
            freed(sp, KR_GROUP % 2, free_count(KR_GROUP))
            swap_halves(0)
            for g in range(HEADS // 2):
                if g + 2 < HEADS // 2:
                    load_q(g + 2)
                else:
                    load_kv(g - 2)
                freed(sp, UQ_GROUP[g] % 2, free_count(UQ_GROUP[g]))
                swap_halves(2 * g + 1)
                if g == 3:
                    load_kv(2)
                swap_halves(2 * g + 2)
            load_kv(3)
            load(wt(pb, 0, KT, 0, WCOL))
            load(wt(pa, 0, KT, 0, WCOL))
            sp.wait_ge(rope_done, 1)
            for g in range(HEADS // 2):
                freed(sp, VT_GROUP[g] % 2, free_count(VT_GROUP[g]))
                for hd in (2 * g, 2 * g + 1):
                    sp.dma_start(kvb[lo:hi, hd, :], kr[lo:hi, :]).then_inc(kr_copied, 16)

            def load_gates(i):
                for br in range(2):
                    sp.dma_start(sig_ab[:, br, :, :],
                                 gates_d[bass.ds(i * 2 + br * DT, 2)].rearrange("a q n -> q a n")
                                 ).then_inc(sig_loaded, 16)

            sp.wait_ge(gate_saved, 16 * 2 * DT)
            sp.wait_ge(y_split, TT)
            load_gates(0)
            with sp.Fori(0, DT // 2 - 1) as i:
                at_.loop(i, 2, 0)
                load(wt(pb, 0, KT, (i + 1) * WCOL, WCOL))
                load(wt(pa, 0, KT, (i + 1) * WCOL, WCOL))
                sp.wait_ge(gated_ready, i + 1)
                load_gates(i + 1)
                at_.end(DT // 2 - 1)
            for q in range(2 * OUT_N):
                load_kn(wo, q * WCOL)
                if q < 2:
                    sp.wait_ge(gated_ready, DT // 2)
                else:
                    freed(sp, (OUT_GROUP + q - 2) % 2, free_count(OUT_GROUP + q - 2))
                sp.dma_start(xs[:, q % 2, :, :], x2.rearrange("(t q) d -> q t d", q=P)
                             [:, :, q * WCOL:(q + 1) * WCOL]).then_inc(xs_loaded[q % 2], 16)
            sp.dma_start(p_tok[:, :, :], p2.rearrange("(t q) d -> q t d", q=P)).then_inc(p_loaded, 16)
            with sp.Fori(0, FFN) as i:
                at_.loop(i, 8, 0)
                for j in range(2):
                    load_kn(f1, i * (CHUNK * P) + j * WCOL)
                for j in range(4):
                    load(f2[bass.ds(i * (CHUNK * P), CHUNK * P), j * WCOL:(j + 1) * WCOL]
                         .rearrange("(k q) c -> q k c", q=P))
                at_.end(FFN)
            for q in range(2 * OUT_N):
                load_kn(pg, q * WCOL)
                load(wt(pw, 0, 2, q * WCOL, WCOL), 2)
            freed(sp, RMS_GROUPS[1] % 2, free_count(RMS_GROUPS[1]))
            sp.dma_start(gfin_row[:, :], g_final.partition_broadcast(P)).then_inc(gfin_loaded, 16)
            for t in range(TT):
                g = FIN_GROUP + t
                freed(sp, g % 2, free_count(g))
                sp.dma_start(out2[t * P:(t + 1) * P, :], tmp[:, t % 2, 0, :]).then_inc(stored[t % 2], 16)
            for s in range(2):
                sp.wait_ge(stored[s], 16 * TT // 2)

        @block.gpsimd
        def _(pool):
            at_ = Place()
            with nc.allow_non_contiguous_dma(reason="gain and position columns, one float per partition"):
                for c, g in ((g_cq_c, g_cq[0]), (g_ckv_c, g_ckv[0]), (g_mlp_c, g_mlp[0]), (g_ple_c, g_ple[0])):
                    pool.dma_start(c, g.rearrange("(k q) -> q k", q=P)).then_inc(const_cols, 16)
                pool.dma_start(pos_ci[:, :], positions[0].rearrange("(t q) -> q t", q=P)).then_inc(const_cols, 16)
            for tl in (ident, ident_b, causal_b):
                pool.memset(tl[:, :], 0.0).then_inc(consts_half, 1)
            pool.memset(ones[:, :], 1.0).then_inc(consts_ready, 1)
            pool.wait_ge(consts_half, 3)
            for tl in (ident, ident_b):
                pool.affine_select(out=tl[:, :], in_=tl[:, :], compare_op=ALU.not_equal, fill=1.0, base=0,
                                   pattern=[[-1, P]], channel_multiplier=1).then_inc(consts_ready, 1)
            pool.affine_select(out=causal_b[:, :], in_=causal_b[:, :], compare_op=ALU.is_ge, fill=NEG, base=0,
                               pattern=[[-1, P]], channel_multiplier=1).then_inc(consts_ready, 1)

            def lo_parts(k):
                for _ in range(k):
                    s, _, num, _ = at_.slab()
                    pool.wait_ge(hi_ready, num + 1)
                    pool.tensor_tensor(w_lo[s][:, :, :], w_raw[s][:, :, :], w_hi[s][:, :, :].bitcast(F32),
                                       ALU.subtract).then_inc(lo_ready, 1)

            lo_parts(2)
            pool.wait_ge(near_dist, SELECT_FROM)
            for i in range(SELECT_FROM):
                diag = sc[:, SC_AT[i] + i * P:SC_AT[i] + KEYS[i]]
                pool.affine_select(out=diag, in_=diag, compare_op=ALU.is_ge, fill=-NEG, base=0,
                                   pattern=[[-1, P]], channel_multiplier=1).then_inc(near_masked, 1)
            lo_parts(4)
            for i in range(SELECT_FROM, TT):
                diag = sc[:, SC_AT[i] + i * P:SC_AT[i] + KEYS[i]]
                pool.wait_ge(rel_used, IDX_HEADS * (i - SELECT_FROM + 1))
                pool.affine_select(out=diag, in_=diag, compare_op=ALU.is_ge, fill=LOWEST, base=0,
                                   pattern=[[-1, P]], channel_multiplier=1).then_inc(far_masked, 1)
            lo_parts(8)

            def latent_lo(c):
                full, dst_lo, dst_hi, total, first, before = LATENTS[c][0:6]
                pool.wait_ge(c_hi, c + 1)
                pool.tensor_tensor(dst_lo, full, dst_hi.bitcast(F32), ALU.subtract).then_inc(c_lo, 1)
                if not first:
                    pool.wait_ge(c_sq, c + 1)
                    if before >= 1:
                        pool.wait_ge(c_sum, before)
                    pool.tensor_tensor(total, total, stage[:, :], ALU.add).then_inc(c_sum, 1)

            latent_lo(0)
            latent_lo(1)
            lo_parts(2)
            latent_lo(2)
            latent_lo(3)
            lo_parts(2)
            latent_lo(4)

            def lo_loop(trips, n):
                with pool.Fori(0, trips) as i:
                    at_.loop(i, n, 0)
                    lo_parts(n)
                    at_.end(trips)

            lo_loop(GATES_N, 4)
            lo_parts(HEADS + 2)
            for k in range(YT):
                pool.wait_ge(yb_hi_done, k + 1)
                pool.tensor_tensor(yb_lo[:, k, :], yb[:, k, :], yb_hi[:, k, :].bitcast(F32),
                                   ALU.subtract).then_inc(yb_split, 1)
            lo_parts(DT - 2)
            for trips, n in ((OUT_N, 4), (FFN, 8), (OUT_N, 6)):
                lo_loop(trips, n)

        @block.scalar
        def _(act):
            at_ = Place()
            ahead = Place()
            steps = [0]

            def link(ins):
                steps[0] += 1
                ins.then_inc(act_step, 1)
                act.wait_ge(act_step, steps[0])

            def hi_parts(k):
                for _ in range(k):
                    s, first, num, filled = ahead.slab()
                    act.wait_ge(raw_loaded[s], filled)
                    if first >= 2:
                        act.wait_ge(slab_used, num - 1)
                    act.activation(w_hi[s][:, :, :], w_raw[s][:, :, :], ACT.Copy).then_inc(hi_ready, 1)

            def group(slabs=0):
                half, done, _, free = at_.group(slabs)
                complete(act, done)
                return half

            def x_hi(t):
                half = group()
                act.activation(n_hi[:, :, t * P:(t + 1) * P],
                               bank(4 * half, 2).rearrange("q (k n) -> q k n", k=DT), ACT.Copy).then_inc(n_hi_done, 1)

            for t in range(TT):
                act.wait_ge(x_loaded[t], 16)
                if t >= 2:
                    act.wait_ge(x_scaled, t - 1)
                act.activation(stage[:, :], x_tok[:, t, :], ACT.Square,
                               accum_out=ss_c[:, t % 2:t % 2 + 1]).then_inc(row_ss, 1)
                act.wait_ge(row_ss, t + 1)
                if t == 0:
                    act.wait_ge(row_ready, 1)
                act.activation(rstd_c[:, t % 2:t % 2 + 1], ss_c[:, t % 2:t % 2 + 1], ACT.Sqrt,
                               bias=eps_c, scale=1.0 / D).then_inc(row_std, 1)
                if t >= 1:
                    x_hi(t - 1)
            hi_parts(2)
            x_hi(TT - 1)
            lo, hi = NOPE, QB_DIM
            act.wait_ge(rope_arg, 1)
            link(act.activation(rope_r[lo:hi, :], rope_r[lo:hi, :], ACT.Sin))
            act.dma_start(rope_d[0], rope_r[lo:hi, :]).then_inc(rope_saved, 16)
            act.wait_ge(rope_arg, 2)
            link(act.activation(stage[lo:hi, :], stage[lo:hi, :], ACT.Sin, scale=inv_c[lo:hi, 1:2]))
            act.dma_start(rope_d[1], stage[lo:hi, :]).then_inc(rope_saved, 16)
            hi_parts(2)
            half = group(2)
            act.activation(qi[:, :, :].rearrange("q a n -> q (a n)"), bank(4 * half, 4), ACT.Copy).then_inc(
                psum_free[half], 1)
            hi_parts(2)
            half = group(2)
            wr = slice(HEAD_DIM, HEAD_DIM + IDX_HEADS)
            act.activation(ki[0:HEAD_DIM, :], tile_ps(half, 0)[0:HEAD_DIM, :], ACT.Copy).then_inc(idx_ready, 1)
            act.activation(ki_wi[wr, :], tile_ps(half, 0)[wr, :], ACT.Copy).then_inc(psum_free[half], 1)
            m = 0
            for i in range(SELECT_FROM, TT):
                for hd in range(IDX_HEADS):
                    act.wait_ge(idx_done, m + 1)
                    if m >= 2:
                        act.wait_ge(rel_used, m - 1)
                    act.activation(rel[:, m % 2, 0:KEYS[i]], bank(2 * (m % 4), 2)[:, 0:KEYS[i]],
                                   ACT.Relu).then_inc(rel_done, 1)
                    m += 1
            for g in range(2):
                hi_parts(2)
                half = group(2)
                for j in range(2):
                    last = act.activation(qa[:, 2 * g + j, :], tile_ps(half, j), ACT.Copy,
                                          scale=q_scale[:, 2 * g + j:2 * g + j + 1])
                last.then_inc(psum_free[half], 1)
            hi_parts(2)
            half = group(2)
            for c in range(KV_HEADS_A):
                r = slice(c * HEAD_DIM, (c + 1) * HEAD_DIM)
                act.activation(ka[r, c, :], tile_ps(half, 0)[r, :], ACT.Copy).then_inc(ka_ready, 1)
            act.activation(va_features[:, :], tile_ps(half, 1), ACT.Copy).then_inc(psum_free[half], 1)

            def latent(c, src, last):
                full, _, _, total, first, before, gain = LATENTS[c]
                if c == 0:
                    act.wait_ge(rel_used, IDX_HEADS * (TT - SELECT_FROM))
                    act.wait_ge(rope_saved, 32)
                if not first and before >= 1:
                    act.wait_ge(c_sum, before)
                act.activation(total if first else stage[:, :], src, ACT.Square).then_inc(c_sq, 1)
                ins = act.activation(full, src, ACT.Copy, scale=gain)
                if last is None:
                    ins.then_inc(c_scaled, 1)
                else:
                    ins.then_inc(psum_free[last], 1)

            def latent_hi(c, last):
                if last is None:
                    act.wait_ge(c_scaled, c // 2 + 1)
                else:
                    freed(act, last, (at_.groups - 1) // 2 + 1)
                act.activation(LATENTS[c][2], LATENTS[c][0], ACT.Copy).then_inc(c_hi, 1)

            hi_parts(2)
            half = group(2)
            latent(0, tile_ps(half, 0), None)
            latent(1, tile_ps(half, 1), half)
            latent_hi(0, None)
            latent_hi(1, half)
            half = group()
            act.activation(va[:, :, :].rearrange("q t n -> q (t n)"), bank(4 * half, 2), ACT.Copy).then_inc(
                psum_free[half], 1)
            hi_parts(2)
            half = group(2)
            latent(2, tile_ps(half, 0), None)
            latent(3, tile_ps(half, 1), half)
            latent_hi(2, None)
            latent_hi(3, half)
            hi_parts(2)
            half = group(2)
            latent(4, tile_ps(half, 0), half)
            latent_hi(4, half)
            act.wait_ge(c_sum, 3)
            with act.Fori(0, GATES_N) as i:
                at_.loop(i, 4, 2)
                ahead.loop(i, 4)
                for j in range(2):
                    hi_parts(2)
                    half, done, _, free = at_.group(2)
                    complete(act, done)
                    for t in range(2):
                        n = 2 * j + t
                        gate = act.activation(stage[:, :], tile_ps(half, t), ACT.Sigmoid)
                        if t == 0:
                            gate.then_inc(gate_ready, 1)
                            act.wait_ge(gate_ready, i * 2 + (j + 1))
                        else:
                            gate.then_inc(psum_free[half], 1)
                            freed(act, half, free)
                        act.dma_start(gates_d[bass.ds(i * 4 + n, 1)].rearrange("a q n -> q (a n)"),
                                      stage[:, :]).then_inc(gate_saved, 16)
                        act.wait_ge(gate_saved, i * 64 + 16 * (n + 1))
                at_.end(GATES_N)
                ahead.end(GATES_N)
            half = group()
            act.activation(rms_c[:, 0, :], tile_ps(half, 0), ACT.Sqrt, bias=eps_c, scale=1.0 / QL)
            act.activation(rms_c[:, 1, :], tile_ps(half, 1), ACT.Sqrt, bias=eps_c, scale=1.0 / KVL).then_inc(
                psum_free[half], 1)
            hi_parts(2)
            half = group(2)
            act.activation(kr[lo:hi, :], tile_ps(half, 0)[lo:hi, :], ACT.Copy)
            act.wait_ge(q_norm_turned, 1)
            act.activation(q_norm, tile_ps(half, 1)[:, 0:TT], ACT.Copy,
                           scale=1.0 / SCALE_B).then_inc(psum_free[half], 1)

            def values(g):
                half = group()
                for j in range(2):
                    hd = 2 * g + j
                    last = act.activation(vb[:, :, hd * HEAD_DIM:(hd + 1) * HEAD_DIM],
                                          bank(4 * half + j).rearrange("q (t n) -> q t n", t=TT), ACT.Copy)
                last.then_inc(psum_free[half], 1)

            for kind, g in LATENT_HEADS:
                if kind == "vt":
                    values(g)
                    continue
                hi_parts(1)
                if kind == "kv":
                    at_.group(1)
                    continue
                half = group(1)
                for j in range(2):
                    last = act.activation(qb[0:QB_DIM, 2 * g + j, :], tile_ps(half, j)[0:QB_DIM, :], ACT.Copy)
                last.then_inc(psum_free[half], 1)

            def copy_probs(n):
                part = copied(n)[1]
                if part:
                    act.wait_ge(pt_ready, n + 1)
                    if n >= 2:
                        act.wait_ge(pv_done, n - 1)
                    r = slice(part[0] * P, part[1] * P)
                    act.activation(prob_t[:, n % 2, r], bank(4, 2)[:, r], ACT.Copy).then_inc(pt_act, 1)

            def y_hi(i):
                act.wait_ge(y_ready, TT + i + 1)
                act.activation(ya_hi[:, :, i * P:(i + 1) * P], y_f32[:, i % 2, :].rearrange("q (k n) -> q k n", k=YT),
                               ACT.Copy).then_inc(y_hi_done, 1)

            def y_b_hi(k):
                act.wait_ge(dist_ready, TT - SELECT_FROM)
                act.wait_ge(y_ready, TT)
                act.activation(yb_hi[:, k, :], yb[:, k, :], ACT.Copy).then_inc(yb_hi_done, 1)

            for n, (br, i, hd) in enumerate(STEPS):
                ti = n // HEADS
                if n >= 2:
                    copy_probs(n - 2)
                act.wait_ge(shift_ready, n + 1)
                if n >= 2:
                    act.wait_ge(pt_ready, n - 1)
                e = KEYS[i]
                src = bank(2 * (n % 2), 2)[:, 0:e] if br == "B" else prob[:, n % 2, 0:e]
                k = (ti % 2) * HEADS + hd
                act.activation(prob[:, n % 2, 0:e], src, ACT.Exp, bias=shift_c[:, n % 4:n % 4 + 1],
                               scale=q_norm[:, i:i + 1] if br == "B" else SLOPES[hd],
                               accum_out=sums[:, k:k + 1]).then_inc(prob_ready, 1)
                if hd == 4 and ti > TT:
                    y_hi(ti - 1 - TT)
                if br == "A" and hd == 6 and i >= B_HI_FROM:
                    y_b_hi(i - B_HI_FROM)
            copy_probs(N - 2)
            copy_probs(N - 1)
            y_hi(TT - 1)

            with act.Fori(0, DT // 2) as i:
                at_.loop(i, 2, 2)
                ahead.loop(i, 2)
                hi_parts(2)
                act.wait_ge(gated_ready, i + 1)
                act.activation(merged_hi[:, bass.ds(i * 2, 2), :].rearrange("q a n -> q (a n)"),
                               gated[:, :, :].rearrange("q a n -> q (a n)"), ACT.Copy).then_inc(m_hi_done, 1)
                at_.group(1)
                at_.group(1)
                at_.end(DT // 2)
                ahead.end(DT // 2)
            def norm_hi_part(gain, k):
                act.activation(n2_hi[:, bass.ds(k, 1), :].rearrange("q a n -> q (a n)"),
                               h[:, bass.ds(k, 1), :].rearrange("q a n -> q (a n)"), ACT.Copy,
                               scale=gain[:, bass.ds(k, 1)]).then_inc(norm_hi, 1)

            with act.Fori(0, OUT_N) as i:
                at_.loop(i, 4, 2, 2)
                ahead.loop(i, 4)
                for j in range(2):
                    hi_parts(2)
                    half, _, _, free = at_.group(2, turn=True)
                    freed(act, half, free)
                    act.activation(gated[:, :, :], h[:, bass.ds(i * 4 + 2 * j, 2), :], ACT.Square).then_inc(h_sq, 1)
                    for t in range(2):
                        norm_hi_part(g_mlp_c, i * 4 + (2 * j + t))
                    act.wait_ge(sq_ready, i * 2 + (j + 2))
                at_.end(OUT_N)
                ahead.end(OUT_N)

            def root():
                half = group()
                act.activation(rms[:, :], tile_ps(half, 0), ACT.Sqrt, bias=eps_c,
                               scale=1.0 / D).then_inc(psum_free[half], 1)

            root()
            half = group()
            act.activation(pt_hi[:, :, :].rearrange("q a n -> q (a n)"), bank(4 * half, 4), ACT.Copy).then_inc(
                pt_hi_done, 1)

            def hidden(i):
                for j in range(2):
                    hi_parts(2)
                    half, _, _, free = at_.group(2)
                    for t in range(2):
                        n = 2 * j + t
                        if t == 0:
                            act.wait_ge(relu_ready, i * 2 + (j + 1))
                        else:
                            freed(act, half, free)
                        act.activation(tmp[:, j, t, :], tmp[:, j, t, :], ACT.Square).then_inc(hid_sq, 1)
                        act.wait_ge(hid_sq, i * 4 + (n + 1))
                        act.activation(hid_hi[:, n, :], tmp[:, j, t, :], ACT.Copy).then_inc(hid_hi_done, 1)

            with act.Fori(0, FFN - 1) as i:
                at_.loop(i, 8, 6)
                ahead.loop(i, 8)
                hidden(i)
                for q in range(4):
                    hi_parts(1)
                    at_.group(1)
                at_.end(FFN - 1)
                ahead.end(FFN - 1)
            hidden(FFN - 1)
            for q in range(4):
                hi_parts(1)
                half, _, _, free = at_.group(1)
                freed(act, half, free)
                for k in (2 * q, 2 * q + 1):
                    if k >= 2:
                        act.wait_ge(sq_ready, SQ3 + k - 1)
                    act.activation(tmp[:, 1, k % 2, :], h[:, k, :], ACT.Square).then_inc(h_sq, 1)
                for k in (2 * q, 2 * q + 1):
                    norm_hi_part(g_ple_c, k)
            root()
            for q in range(2 * OUT_N):
                hi_parts(2 if q < 3 else 1)
                half, _, _, free = at_.group(2)
                act.wait_ge(gate_in, q + 1)
                freed(act, half, free)
                act.activation(tmp[:, q % 2, :, :], tmp[:, q % 2, :, :], ACT.Sigmoid).then_inc(gate_fn, 1)
                at_.group(1)
                if q < 3:
                    hi_parts(1)
            for t in range(TT):
                half = group()
                if t >= 2:
                    freed(act, half, free_count(FIN_GROUP + t - 2))
                act.activation(tmp[:, t % 2, 1, :], bank(4 * half, 2), ACT.Square,
                               accum_out=ss_c[:, t % 2:t % 2 + 1]).then_inc(fin_ss, 1)
                act.wait_ge(fin_ss, t + 1)
                act.activation(rstd_c[:, t % 2:t % 2 + 1], ss_c[:, t % 2:t % 2 + 1], ACT.Sqrt,
                               bias=eps_c, scale=1.0 / D).then_inc(fin_std, 1)

        @block.vector
        def _(dve):
            at_ = Place()
            steps = [0]

            def link(ins):
                steps[0] += 1
                ins.then_inc(dve_step, 1)
                dve.wait_ge(dve_step, steps[0])

            def group(slabs=0, turn=False):
                half, done, _, free = at_.group(slabs, turn)
                complete(dve, done)
                return half

            dve.memset(eps_c, EPS).then_inc(row_ready, 1)
            link(dve.memset(rows[0:1, :, :], 0.0))
            half_rope = ROPE // 2
            for j in range(half_rope):
                dve.memset(rows[0:1, 0, NOPE + j:NOPE + j + half_rope + 1:half_rope], THETA ** (-j / half_rope))
            dve.memset(rows[0:1, 1, NOPE:NOPE + half_rope], -1.0)
            dve.memset(rows[0:1, 1, NOPE + half_rope:QB_DIM], 1.0).then_inc(row_ready, 1)
            for t in range(YT):
                for j in range(2):
                    dve.memset(q_scale[j * HEAD_DIM:(j + 1) * HEAD_DIM, t:t + 1], SCALE_A / SLOPES[2 * t + j])

            def x_lo(t):
                half, _, _, _ = at_.group()
                dve.wait_ge(n_hi_done, t + 1)
                dve.tensor_tensor(n_lo[:, :, t * P:(t + 1) * P],
                                  bank(4 * half, 2).rearrange("q (k n) -> q k n", k=DT),
                                  n_hi[:, :, t * P:(t + 1) * P].bitcast(F32), ALU.subtract).then_inc(psum_free[half], 1)

            dve.wait_ge(gains_loaded, 16)
            dve.wait_ge(col_done, 1)
            dve.tensor_copy(inv_c[0:QB_DIM, :], bank(2)[0:QB_DIM, 0:2]).then_inc(inv_copied, 1)
            for t in range(TT):
                dve.wait_ge(row_std, t + 1)
                r = rstd_c[:, t % 2:t % 2 + 1]
                link(dve.reciprocal(r, r))
                dve.scalar_tensor_tensor(x_tok[:, t, :], x_tok[:, t, :], r, gmix_row[:, :], ALU.mult,
                                         ALU.mult).then_inc(x_scaled, 1)
                if t >= 1:
                    x_lo(t - 1)
            x_lo(TT - 1)

            dve.wait_ge(pos_loaded, 16)
            dve.wait_ge(const_cols, 16 * 5)
            link(dve.tensor_copy(pos_f[:, :], pos_i[:, :]))
            dve.wait_ge(x_scaled, TT)
            link(dve.tensor_scalar(neg_pos, pos_ci[:, :], -1.0, None, ALU.mult))

            def distances(i):
                d = sc[:, SC_AT[i]:SC_AT[i] + KEYS[i]]
                link(dve.tensor_scalar(d, pos_f[:, 0:KEYS[i]], neg_pos[:, i:i + 1], None, ALU.add))
                return dve.scalar_tensor_tensor(d, d, -1.0, d, ALU.mult, ALU.max)

            for i in range(SELECT_FROM):
                distances(i).then_inc(near_dist, 1)
            lo, hi = NOPE, QB_DIM
            ang, turns = rope_a[lo:hi, :], rope_k[lo:hi, :]
            link(dve.tensor_scalar(ang, pos_f[lo:hi, :], inv_c[lo:hi, 0:1], None, ALU.mult))
            for arg, quarter in ((rope_r[lo:hi, :], 0.25), (stage[lo:hi, :], 0.0)):
                link(dve.tensor_scalar(turns, ang, 0.15915494309189535, quarter, ALU.mult, ALU.add))
                link(dve.tensor_scalar(turns, turns, ROUND_MAGIC, None, ALU.add))
                link(dve.tensor_scalar(turns, turns, -ROUND_MAGIC, None, ALU.add))
                link(dve.scalar_tensor_tensor(arg, turns, -TWO_PI_1, ang, ALU.mult, ALU.add))
                link(dve.scalar_tensor_tensor(arg, turns, -TWO_PI_2, arg, ALU.mult, ALU.add))
                link(dve.scalar_tensor_tensor(arg, turns, -TWO_PI_3, arg, ALU.mult, ALU.add))
                link(dve.tensor_scalar(arg, arg, quarter * 2 * 3.141592653589793, PI, ALU.add, ALU.min))
                dve.tensor_scalar(arg, arg, -PI, None, ALU.max).then_inc(rope_arg, 1)
            for slabs in [2] * 6 + [0] + [2] * (2 + 2 * GATES_N) + [0] + [2]:
                at_.group(slabs)
            assert at_.groups == KR_GROUP + 1

            dve.wait_ge(wi_done, 1)
            dve.tensor_scalar(w_tok[:, :, :].rearrange("q t h -> q (t h)"), bank(7)[:, 0:TT * IDX_HEADS],
                              (IDX_HEADS * HEAD_DIM) ** -0.5, None, ALU.mult).then_inc(wi_copied, 1)
            dve.wait_ge(wi_copied, 1)
            m = 0
            for i in range(SELECT_FROM, TT):
                s_i = sc[:, SC_AT[i]:SC_AT[i] + KEYS[i]]
                for hd in IDX_ORDER:
                    dve.wait_ge(rel_done, m + 1)
                    if hd == IDX_ORDER[0]:
                        ins = dve.tensor_scalar(s_i, rel[:, m % 2, 0:KEYS[i]], w_tok[:, i, hd:hd + 1], None, ALU.mult)
                    else:
                        dve.wait_ge(rel_used, m)
                        ins = dve.scalar_tensor_tensor(s_i, rel[:, m % 2, 0:KEYS[i]], w_tok[:, i, hd:hd + 1], s_i,
                                                       ALU.mult, ALU.add)
                    ins.then_inc(rel_used, 1)
                    m += 1

            def select(i, r, buffers, before=None):
                e = KEYS[i]
                s_i, (work, eq, rank) = sc[:, SC_AT[i]:SC_AT[i] + e], (b[:, 0:e] for b in buffers)
                bar = top8[:, 7:8]
                left = s_i if r < 2 else (before or buffers)[0][:, 0:e]
                if r == 0:
                    dve.wait_ge(far_masked, i - SELECT_FROM + 1)
                if r < ROUNDS and r % 2 == 0:
                    link(dve.max(top8, left))
                elif r < ROUNDS:
                    link(dve.match_replace(work, top8, left, LOWEST))
                elif r == ROUNDS:
                    link(dve.tensor_scalar(work, s_i, bar, None, ALU.is_gt, ALU.add, accum_out=need_c))
                    link(dve.tensor_scalar(need_c, need_c, -1.0, float(TOPK), ALU.mult, ALU.add))
                elif r == ROUNDS + 1:
                    link(dve.tensor_scalar(eq, s_i, bar, None, ALU.is_equal))
                elif r == ROUNDS + 2:
                    link(dve.tensor_tensor_scan(rank, eq, eq, 0.0, ALU.add, ALU.max))
                elif r == ROUNDS + 3:
                    link(dve.scalar_tensor_tensor(eq, rank, need_c, eq, ALU.is_le, ALU.mult))
                elif r == ROUNDS + 4:
                    link(dve.tensor_tensor(work, work, eq, ALU.add))
                elif r == ROUNDS + 5:
                    link(dve.tensor_scalar(work, work, 0.0, -NEG, ALU.is_equal, ALU.mult))
                elif r == ROUNDS + 6:
                    link(dve.tensor_scalar(s_i, pos_f[:, 0:e], neg_pos[:, i:i + 1], None, ALU.add))
                elif r == ROUNDS + 7:
                    link(dve.scalar_tensor_tensor(s_i, s_i, -1.0, s_i, ALU.mult, ALU.max))
                else:
                    dve.tensor_tensor(s_i, s_i, work, ALU.add).then_inc(dist_ready, 1)

            dve.wait_ge(rope_saved, 32)
            for i in range(SELECT_FROM, TT - 1):
                for r in range(PASSES):
                    select(i, r, tk_early)

            for r in range(LAST_EARLY):
                select(TT - 1, r, tk_early)
                if r == 2:
                    freed(dve, SUM_GROUP % 2, free_count(SUM_GROUP))
                    link(dve.reciprocal(rms_c[:, 1, :], rms_c[:, 1, :]))
            def rope(n):
                rows_, sw = ROPES[n][lo:hi, :], swap[n % 2][lo:hi, :]
                dve.wait_ge(swap_loaded[n % 2], 32 * (n // 2 + 1))
                link(dve.tensor_tensor(sw, sw, rope_sin[lo:hi, :], ALU.mult))
                link(dve.tensor_tensor(rows_, rows_, rope_cos[lo:hi, :], ALU.mult))
                dve.tensor_tensor(rows_, rows_, sw, ALU.add).then_inc(rope_done, 1)

            for kind, g in LATENT_HEADS:
                if kind == "q":
                    half, _, _, free = at_.group(1)
                    if g == 0:
                        freed(dve, KR_GROUP % 2, free_count(KR_GROUP))
                        link(dve.reciprocal(q_norm, q_norm))
                        dve.wait_ge(table_loaded, 32)
                        rope(0)
                    if g < HEADS // 2 - 1:
                        rope(2 * g + 1)
                        rope(2 * g + 2)
                    else:
                        freed(dve, half, free)
                        select(TT - 1, LAST_EARLY, tk_late, before=tk_early)
                elif kind == "kv":
                    half = group(1)
                    for j in range(2):
                        last = dve.tensor_tensor(kvb[:, 2 * g + j, :], tile_ps(half, j), rms_c[:, 1, :], ALU.mult)
                    last.then_inc(psum_free[half], 1)
                    if g < 2:
                        rope(HEADS - 1 + g)
                    elif g == HEADS // 2 - 1:
                        for r in range(AFTER_KEYS):
                            select(TT - 1, LAST_EARLY + 1 + r, tk_late)
                else:
                    at_.group()

            def copy_probs(n):
                part = copied(n)[0]
                if part:
                    dve.wait_ge(pt_ready, n + 1)
                    if n >= 2:
                        dve.wait_ge(pv_done, n - 1)
                    r = slice(part[0] * P, part[1] * P)
                    dve.tensor_copy(prob_t[:, n % 2, r], bank(4, 2)[:, r]).then_inc(pt_dve, 1)

            def y_factors(ti):
                k = (ti % 2) * HEADS
                dve.wait_ge(prob_ready, HEADS * (ti + 1))
                link(dve.reciprocal(inv_sum, sums[:, k:k + HEADS]))
                dve.tensor_copy(y_f32[:, ti % 2, :].rearrange("q (h d) -> q h d", h=HEADS),
                                inv_sum.unsqueeze(2).to_broadcast([P, HEADS, HEAD_DIM])).then_inc(y_factor_ready, 1)

            def y_out(ti):
                dve.wait_ge(yt_ready, ti + 1)
                link(dve.tensor_copy(y_f32[:, ti % 2, :], bank(7)))
                dve.wait_ge(pv_done, HEADS * (ti + 1))
                if ti < TT:
                    dve.tensor_tensor(yb[:, :, ti * P:(ti + 1) * P], bank(6).rearrange("q (k n) -> q k n", k=YT),
                                      y_f32[:, ti % 2, :].rearrange("q (k n) -> q k n", k=YT),
                                      ALU.mult).then_inc(y_ready, 1)
                else:
                    dve.tensor_tensor(y_f32[:, ti % 2, :], bank(6), y_f32[:, ti % 2, :], ALU.mult).then_inc(y_ready, 1)

            def y_lo(i):
                r = slice(i * P, (i + 1) * P)
                dve.wait_ge(y_hi_done, i + 1)
                dve.tensor_tensor(ya_lo[:, :, r], y_f32[:, i % 2, :].rearrange("q (k n) -> q k n", k=YT),
                                  ya_hi[:, :, r].bitcast(F32), ALU.subtract).then_inc(y_split, 1)

            for n, (br, i, hd) in enumerate(STEPS):
                ti = n // HEADS
                e = KEYS[i]
                top, shift = max_c[:, n % 4:n % 4 + 1], shift_c[:, n % 4:n % 4 + 1]
                if br == "A":
                    copy_probs(n - 2)
                dve.wait_ge(s_ready, n + 1)
                if br == "B":
                    link(dve.tensor_reduce(top, bank(2 * (n % 2), 2)[:, 0:e], AXIS.X, ALU.max))
                    dve.tensor_scalar(shift, top, q_norm[:, i:i + 1], -1.0, ALU.mult,
                                      ALU.mult).then_inc(shift_ready, 1)
                else:
                    dve.wait_ge(pt_ready, n - 1)
                    if n == HEADS * TT:
                        dve.wait_ge(near_masked, SELECT_FROM)
                    link(dve.tensor_tensor_reduce(prob[:, n % 2, 0:e], bank(2 * (n % 2), 2)[:, 0:e],
                                                  sc[:, SC_AT[i]:SC_AT[i] + e], 1.0, LOWEST, ALU.subtract, ALU.max,
                                                  top))
                    dve.tensor_scalar(shift, top, -SLOPES[hd], None, ALU.mult).then_inc(shift_ready, 1)
                if hd == 2 and ti >= 1:
                    y_out(ti - 1)
                if br == "B" and n >= 2:
                    copy_probs(n - 2)
                if hd == 1 and ti >= 1:
                    y_factors(ti - 1)
                if hd == 5 and ti > TT:
                    y_lo(ti - 1 - TT)
                if n in LATE_STEPS:
                    select(TT - 1, PASSES - len(LATE_STEPS) + LATE_STEPS.index(n), tk_late)
            copy_probs(N - 2)
            y_factors(2 * TT - 1)
            copy_probs(N - 1)
            y_out(2 * TT - 1)
            y_lo(TT - 1)

            with dve.Fori(0, DT // 2) as i:
                at_.loop(i, 2, 2)
                both = gated[:, :, :].rearrange("q a n -> q (a n)")
                siga, sigb = (sig_ab[:, b, :, :].rearrange("q a n -> q (a n)") for b in range(2))
                half = group(1)
                dve.wait_ge(sig_loaded, i * 32 + 32)
                dve.tensor_tensor(both, bank(4 * half, 4), sigb, ALU.mult).then_inc(psum_free[half], 1)
                half, done, _, free = at_.group(1)
                complete(dve, done)
                dve.tensor_tensor(siga, bank(4 * half, 4), siga, ALU.mult).then_inc(psum_free[half], 1)
                freed(dve, half, free)
                dve.tensor_tensor(both, both, siga, ALU.add).then_inc(gated_ready, 1)
                dve.wait_ge(m_hi_done, i + 1)
                dve.tensor_tensor(merged_lo[:, bass.ds(i * 2, 2), :].rearrange("q a n -> q (a n)"), both,
                                  merged_hi[:, bass.ds(i * 2, 2), :].rearrange("q a n -> q (a n)").bitcast(F32),
                                  ALU.subtract).then_inc(m_lo_done, 1)
                dve.wait_ge(m_lo_done, i + 1)
                at_.end(DT // 2)
            dve.memset(sq_sum[:, :], 0.0).then_inc(sq_ready, 1)
            with dve.Fori(0, OUT_N) as i:
                at_.loop(i, 4, 2, 2)
                for j in range(2):
                    half = group(2, turn=True)
                    dve.tensor_copy(h[:, bass.ds(i * 4 + 2 * j, 2), :].rearrange("q a n -> q (a n)"),
                                    bank(4 * half, 4)).then_inc(psum_free[half], 1)
                    dve.wait_ge(h_sq, i * 2 + (j + 1))
                    dve.tensor_tensor(gated[:, 0, :], gated[:, 0, :], gated[:, 1, :], ALU.add).then_inc(sq_pair, 1)
                    dve.wait_ge(sq_pair, i * 2 + (j + 1))
                    dve.wait_ge(sq_ready, i * 2 + (j + 1))
                    dve.tensor_tensor(sq_sum[:, :], sq_sum[:, :], gated[:, 0, :], ALU.add).then_inc(sq_ready, 1)
                at_.end(OUT_N)

            def inverse():
                at_.group()
                g = at_.groups - 1
                freed(dve, g % 2, free_count(g))
                link(dve.reciprocal(rms[:, :], rms[:, :]))

            def norm_lo_part(gain, before, k):
                dve.wait_ge(norm_hi, before + k + 1)
                dve.scalar_tensor_tensor(n2_lo[:, k, :], h[:, k, :], gain[:, k:k + 1],
                                         n2_hi[:, k, :].bitcast(F32), ALU.mult, ALU.subtract).then_inc(norm_lo, 1)

            for k in range(DT):
                norm_lo_part(g_mlp_c, 0, k)
            inverse()
            half, _, _, _ = at_.group()
            dve.wait_ge(pt_hi_done, 1)
            dve.tensor_tensor(pt_lo[:, :, :].rearrange("q a n -> q (a n)"), bank(4 * half, 4),
                              pt_hi[:, :, :].rearrange("q a n -> q (a n)").bitcast(F32),
                              ALU.subtract).then_inc(psum_free[half], 1)

            def hidden(i):
                for j in range(2):
                    half = group(2)
                    for t in range(2):
                        dve.scalar_tensor_tensor(tmp[:, j, t, :], tile_ps(half, t), 0.0, rms[:, :], ALU.max,
                                                 ALU.mult).then_inc(relu_ready if t == 0 else psum_free[half], 1)
                    for t in range(2):
                        n = 2 * j + t
                        dve.wait_ge(hid_hi_done, i * 4 + (n + 1))
                        dve.tensor_tensor(hid_lo[:, n, :], tmp[:, j, t, :], hid_hi[:, n, :].bitcast(F32),
                                          ALU.subtract).then_inc(hid_lo_done, 1)

            def add_out(q):
                half = group(1)
                pair = h[:, 2 * q:2 * q + 2, :].rearrange("q a n -> q (a n)")
                dve.tensor_tensor(pair, pair, bank(4 * half, 4), ALU.add).then_inc(psum_free[half], 1)

            with dve.Fori(0, FFN - 1) as i:
                at_.loop(i, 8, 6)
                hidden(i)
                for q in range(4):
                    add_out(q)
                at_.end(FFN - 1)
            hidden(FFN - 1)
            for q in range(4):
                add_out(q)
                for k in (2 * q, 2 * q + 1):
                    dve.wait_ge(h_sq, 4 + k + 1)
                    if k >= 1:
                        dve.wait_ge(sq_ready, SQ3 + k)
                        dve.tensor_tensor(sq_sum[:, :], sq_sum[:, :], tmp[:, 1, k % 2, :], ALU.add).then_inc(sq_ready, 1)
                    else:
                        dve.tensor_copy(sq_sum[:, :], tmp[:, 1, k % 2, :]).then_inc(sq_ready, 1)
                for k in (2 * q, 2 * q + 1):
                    norm_lo_part(g_ple_c, DT, k)
            inverse()
            for q in range(2 * OUT_N):
                half = group(2)
                for t in range(2):
                    dve.tensor_tensor(tmp[:, q % 2, t, :], tile_ps(half, t), rms[:, :], ALU.mult).then_inc(
                        gate_in if t == 0 else psum_free[half], 1)
                half = group(1)
                gate = tmp[:, q % 2, :, :].rearrange("q a n -> q (a n)")
                pair = h[:, 2 * q:2 * q + 2, :].rearrange("q a n -> q (a n)")
                dve.wait_ge(gate_fn, q + 1)
                dve.tensor_tensor(gate, gate, bank(4 * half, 4), ALU.mult).then_inc(psum_free[half], 1)
                freed(dve, half, free_count(at_.groups - 1))
                dve.tensor_tensor(pair, pair, gate, ALU.add).then_inc(h_final, 1)
            dve.wait_ge(gfin_loaded, 16)
            for t in range(TT):
                half, _, _, _ = at_.group()
                r = rstd_c[:, t % 2:t % 2 + 1]
                dve.wait_ge(fin_std, t + 1)
                link(dve.reciprocal(r, r))
                if t >= 2:
                    dve.wait_ge(stored[t % 2], 16 * (t // 2))
                dve.scalar_tensor_tensor(tmp[:, t % 2, 0, :], bank(4 * half, 2), r, gfin_row[:, :], ALU.mult,
                                         ALU.mult).then_inc(psum_free[half], 1)

        @block.tensor
        def _(pe):
            at_ = Place()

            def group():
                half, _, before, _ = at_.group()
                freed(pe, half, before)
                return half

            def product(half, tiles, slabs, moving, k_of=None, open_=False, first_wait=None):
                total = sum(nk for nk in slabs)
                k = 0
                for nk in slabs:
                    s, _, num, _ = at_.slab()
                    pe.wait_ge(lo_ready, num + 1)
                    for kk in range(nk):
                        if first_wait:
                            first_wait(k)
                        xh, xl = moving(k)
                        for j, (c, w) in enumerate(tiles):
                            wh, wl = w_hi[s][:, kk, c:c + w], w_lo[s][:, kk, c:c + w]
                            for wm, xm, a, z in ((wh, xh, True, False), (wh, xl, False, False), (wl, xh, False, True)):
                                for t in range(2):
                                    last = pe.matmul(bank(4 * half + 2 * j + t)[0:w, :], wm,
                                                     xm[:, t * HALF:(t + 1) * HALF],
                                                     start=(k == 0 and a), stop=(k == total - 1 and z and not open_))
                        k += 1
                    last.then_inc(slab_used, 1)

            FULL = ((0, P), (P, P))
            normed = lambda k: (n_hi[:, k, :], n_lo[:, k, :])

            residual = lambda k: (n2_hi[:, k, :], n2_lo[:, k, :])

            def project(tiles=FULL, wait=None, moving=normed):
                half = group()
                product(half, tiles, (KT, KT), moving, first_wait=wait)

            pe.wait_ge(consts_ready, 4)
            pe.wait_ge(row_ready, 2)
            for c in range(2):
                last = pe.matmul(bank(2)[0:QB_DIM, c:c + 1], rows[0:1, c, 0:QB_DIM], ones[0:1, 0:1],
                                 start=True, stop=True)
            last.then_inc(col_done, 1)
            for t in range(TT):
                half = group()
                pe.wait_ge(x_scaled, t + 1)
                for k in range(DT):
                    last = pe.transpose(bank(4 * half, 2)[:, k * P:(k + 1) * P], x_tok[:, t, k * P:(k + 1) * P],
                                        ident[:, :])
                last.then_inc(turn_done, 1)
            freed(pe, (TT - 1) % 2, TT // 2)
            pe.wait_ge(inv_copied, 1)
            project()
            project(((0, HEAD_DIM + IDX_HEADS),))
            for half in range(2):
                freed(pe, half, at_.groups // 2)
            for t in range(TT):
                last = pe.transpose(bank(7)[:, t * IDX_HEADS:(t + 1) * IDX_HEADS],
                                    ki_wi[HEAD_DIM:HEAD_DIM + IDX_HEADS, t * P:(t + 1) * P],
                                    ident[HEAD_DIM:HEAD_DIM + IDX_HEADS, HEAD_DIM:HEAD_DIM + IDX_HEADS])
            last.then_inc(wi_done, 1)
            m = 0
            for i in range(SELECT_FROM, TT):
                for hd in IDX_ORDER:
                    if hd % 2 == 1:
                        pe.wait_ge(ki_copied, 16)
                    if m == 3:
                        pe.wait_ge(wi_copied, 1)
                    if m >= 4:
                        pe.wait_ge(rel_done, m - 3)
                    r = slice((hd % 2) * HEAD_DIM, (hd % 2 + 1) * HEAD_DIM)
                    for c in range(0, KEYS[i], HALF):
                        e = min(HALF, KEYS[i] - c)
                        last = pe.matmul(bank(2 * (m % 4) + c // HALF)[:, 0:e], qi[r, hd // 2, i * P:(i + 1) * P],
                                         ki[r, c:c + e], start=True, stop=True)
                    last.then_inc(idx_done, 1)
                    m += 1
            pe.wait_ge(rel_done, m)
            for _ in range(4):
                project()
            half = group()
            freed(pe, VA_GROUP % 2, (VA_GROUP - 2) // 2 + 1)
            for t in range(TT):
                last = pe.transpose(bank(4 * half, 2)[:, t * P:(t + 1) * P], va_features[:, t * P:(t + 1) * P], ident[:, :])
            last.then_inc(turn_done, 1)
            project()
            project(((0, P),))
            with pe.Fori(0, GATES_N) as i:
                at_.loop(i, 4, 2, 2)
                project()
                project()
                at_.end(GATES_N)
            half = group()
            pe.wait_ge(c_sum, 3)
            pe.wait_ge(c_sq, QT + KVT)
            for c in range(2):
                for t in range(2):
                    last = pe.matmul(bank(4 * half + 2 * c + t), ones[:, :], rms_c[:, c, t * HALF:(t + 1) * HALF],
                                     start=True, stop=True)
            last.then_inc(turn_done, 1)
            project(((0, QB_DIM),))
            freed(pe, SUM_GROUP % 2, free_count(SUM_GROUP))
            for t in range(TT):
                last = pe.matmul(tile_ps((at_.groups - 1) % 2, 1)[:, t:t + 1], rms_c[0:1, 0, t * P:(t + 1) * P],
                                 ones[0:1, 0:1], start=True, stop=True)
            last.then_inc(q_norm_turned, 1)
            pe.wait_ge(c_lo, QT + KVT)
            for kind, g in LATENT_HEADS:
                half = group()
                if kind == "kv":
                    product(half, FULL, (KVT,), lambda k: (ckv_hi[:, k, :], ckv_lo[:, k, :]))
                elif kind == "q":
                    product(half, ((0, QB_DIM), (QB_DIM, QB_DIM)), (QT,),
                            lambda k: (cq_hi[:, k, :], cq_lo[:, k, :]))
                else:
                    freed(pe, KV_GROUP[g] % 2, free_count(KV_GROUP[g]))
                    for j in range(2):
                        for t in range(TT):
                            last = pe.transpose(bank(4 * half + j)[:, t * HEAD_DIM:(t + 1) * HEAD_DIM],
                                                kvb[HEAD_DIM:P, 2 * g + j, t * P:(t + 1) * P],
                                                ident[HEAD_DIM:P, HEAD_DIM:P])
                    last.then_inc(turn_done, 1)

            for half in range(2):
                freed(pe, half, (at_.groups + 1 - half) // 2)
            pe.wait_ge(kr_copied, 16 * HEADS)
            pe.wait_ge(rope_done, HEADS + 1)
            pe.wait_ge(ka_copied, 32)

            def scores(n):
                br, i, hd = STEPS[n]
                b = 2 * (n % 2)
                if n >= 2:
                    if STEPS[n - 2][0] == "B":
                        pe.wait_ge(prob_ready, n - 1)
                    else:
                        pe.wait_ge(shift_ready, n - 1)
                q = slice(i * P, (i + 1) * P)
                if br == "B":
                    lhs, rhs = qb[0:QB_DIM, hd, q], kvb[0:QB_DIM, hd, :]
                else:
                    r = slice((hd % 2) * HEAD_DIM, (hd % 2 + 1) * HEAD_DIM)
                    lhs, rhs = qa[r, hd // 2, q], ka[r, hd // (HEADS // KV_HEADS_A), :]
                for c in range(0, KEYS[i], HALF):
                    e = min(HALF, KEYS[i] - c)
                    final = c + e == KEYS[i]
                    last = pe.matmul(bank(b + c // HALF)[:, 0:e], lhs, rhs[:, c:c + e], start=True,
                                     stop=not (final and br == "B"))
                if br == "B":
                    last = pe.matmul(bank(b, 2)[:, i * P:(i + 1) * P], ident_b[:, :], causal_b[:, :],
                                     start=False, stop=True)
                last.then_inc(s_ready, 1)

            def turn_probs(n):
                br, i, hd = STEPS[n]
                pe.wait_ge(prob_ready, n + 1)
                if n >= 1:
                    pe.wait_ge(pt_dve, copies(0, n))
                    if copies(1, n):
                        pe.wait_ge(pt_act, copies(1, n))
                for k in range(i + 1):
                    last = pe.transpose(bank(4, 2)[:, k * P:(k + 1) * P], prob[:, n % 2, k * P:(k + 1) * P], ident[:, :])
                last.then_inc(pt_ready, 1)

            def sum_values(n):
                br, i, hd = STEPS[n]
                ti = n // HEADS
                pe.wait_ge(pt_dve, copies(0, n + 1))
                if copies(1, n + 1):
                    pe.wait_ge(pt_act, copies(1, n + 1))
                if hd == 0 and ti >= 1:
                    pe.wait_ge(y_ready, ti)
                c = hd // (HEADS // KV_HEADS_A)
                for k in range(i + 1):
                    v = vb[:, k, hd * HEAD_DIM:(hd + 1) * HEAD_DIM] if br == "B" else \
                        va[:, k, c * HEAD_DIM:(c + 1) * HEAD_DIM]
                    last = pe.matmul(bank(6)[(hd % 2) * HEAD_DIM:(hd % 2 + 1) * HEAD_DIM,
                                             hd // 2 * P:(hd // 2 + 1) * P],
                                     v, prob_t[:, n % 2, k * P:(k + 1) * P], start=(k == 0), stop=(k == i))
                last.then_inc(pv_done, 1)

            def turn_y(ti):
                pe.wait_ge(y_factor_ready, ti + 1)
                for k in range(YT):
                    last = pe.transpose(bank(7)[:, k * P:(k + 1) * P], y_f32[:, ti % 2, k * P:(k + 1) * P], ident[:, :])
                last.then_inc(yt_ready, 1)

            scores(0)
            for n, (br, i, hd) in enumerate(STEPS):
                if n + 1 < N:
                    scores(n + 1)
                if n >= 1:
                    turn_probs(n - 1)
                if n >= 2:
                    sum_values(n - 2)
                if hd == 1 and n >= HEADS:
                    turn_y(n // HEADS - 1)
            turn_probs(N - 1)
            sum_values(N - 2)
            turn_y(2 * TT - 1)
            sum_values(N - 1)

            pe.wait_ge(yb_split, YT)
            pe.wait_ge(y_ready, 2 * TT)
            with pe.Fori(0, DT // 2) as i:
                at_.loop(i, 2, 2, 2)
                for yh, yl in ((yb_hi, yb_lo), (ya_hi, ya_lo)):
                    half = group()
                    if yh is ya_hi:
                        pe.wait_ge(y_split, TT)
                    product(half, FULL, (KT,), lambda k: (yh[:, k, :], yl[:, k, :]))
                at_.end(DT // 2)
            with pe.Fori(0, OUT_N) as i:
                at_.loop(i, 4, 2, 2)
                for j in range(2):
                    half = group()
                    product(half, FULL, (KT, KT), lambda k: (merged_hi[:, k, :], merged_lo[:, k, :]), open_=True,
                            first_wait=lambda k: pe.wait_ge(m_lo_done, k // 2 + 1))
                    pe.wait_ge(xs_loaded[j], i * 16 + 16)
                    for c in range(2):
                        for t in range(TT):
                            last = pe.matmul(bank(4 * half + 2 * c, 2)[:, t * P:(t + 1) * P],
                                             xs[:, j, t, c * P:(c + 1) * P], ident[:, :], start=False,
                                             stop=(t % 4 == 3))
                    last.then_inc(turn_done, 1)
                at_.end(OUT_N)

            def square_sums():
                for t in range(2):
                    last = pe.matmul(bank(4 * half + t), ones[:, :], sq_sum[:, t * HALF:(t + 1) * HALF],
                                     start=True, stop=True)
                last.then_inc(turn_done, 1)

            half = group()
            pe.wait_ge(sq_ready, 2 * OUT_N + 1)
            square_sums()
            half = group()
            pe.wait_ge(p_loaded, 16)
            for f in range(2):
                for t in range(TT):
                    last = pe.transpose(bank(4 * half + 2 * f, 2)[:, t * P:(t + 1) * P], p_tok[:, t, f * P:(f + 1) * P],
                                        ident[:, :])
            last.then_inc(turn_done, 1)
            with pe.Fori(0, FFN) as i:
                at_.loop(i, 8, 6, 6)
                project(wait=lambda k: pe.wait_ge(norm_lo, k + 1), moving=residual)
                project(moving=residual)

                def hid_there(k):
                    pe.wait_ge(hid_lo_done, i * 4 + (k + 1))

                for q in range(4):
                    half = group()
                    product(half, FULL, (KT,), lambda k: (hid_hi[:, k, :], hid_lo[:, k, :]),
                            first_wait=hid_there if q == 0 else None)
                at_.end(FFN)
            half = group()
            pe.wait_ge(sq_ready, SQ3 + DT)
            square_sums()
            for q in range(2 * OUT_N):
                project(wait=(lambda k: pe.wait_ge(norm_lo, DT + k + 1)) if q == 0 else None, moving=residual)
                half = group()
                product(half, FULL, (2,), lambda k: (pt_hi[:, k, :], pt_lo[:, k, :]))
            pe.wait_ge(h_final, 2 * OUT_N)
            for t in range(TT):
                half = group()
                for k in range(DT):
                    last = pe.transpose(bank(4 * half, 2)[:, k * P:(k + 1) * P], h[:, k, t * P:(t + 1) * P], ident[:, :])
                last.then_inc(turn_done, 1)


_INS = ['x', 'p', 'positions', 'g_mix', 'w_in', 'g_cq', 'w_uq', 'g_ckv', 'w_ukv', 'w_pa', 'w_pb', 'w_out', 'g_mlp',
        'w_ff1', 'w_ff2', 'g_ple', 'w_ple_gate', 'w_ple', 'g_final']


def kernel(**inputs):
    import numpy as _np
    import concourse.bacc as _bacc
    from concourse import mybir as _mybir
    from concourse.bass_utils import run_bass_kernel_spmd as _run

    nc = _bacc.Bacc("TRN2", target_bir_lowering=False, num_devices=1)
    arrays, args = {}, []
    for name in _INS:
        a = _np.ascontiguousarray(inputs[name])
        arrays[f"in_{name}_dram"] = a
        args.append(nc.dram_tensor(f"in_{name}_dram", a.shape, _mybir.dt.from_np(a.dtype), kind="ExternalInput").ap())
    args.append(nc.dram_tensor("out_0_dram", inputs["x"].shape, _mybir.dt.float32, kind="ExternalOutput").ap())
    build(nc, *args)
    r = _run(nc, [arrays], core_ids=[0])
    return r.results[0]["out_0_dram"]
```
